# Optimizing a Trainium2 kernel written in Bass

```python
import functools
import jax
import jax.numpy as jnp
from jax import lax
import numpy as np

D_MODEL = 1024
BATCH = 1
SEQ = 1024
DEPTH = 2

GRID_W = 64
CTX_LEN = 256
HEAD_DIM = 64
N_EVEN = (DEPTH + 1) // 2
N_ODD = DEPTH // 2

NA_HEADS = 8
NA_WIN_H_MAX = 8
NA_WIN_W = 16
NA_WIDTH = NA_HEADS * HEAD_DIM
GLA_HEADS = 4
GLA_DK = 64
GLA_DV = 128
GLA_KW = GLA_HEADS * GLA_DK
GLA_VW = GLA_HEADS * GLA_DV
GLA_GATE_RANK = 16
GLA_TAU = 16.0
GLA_CHUNK = 64
AB_SIZES = (NA_WIDTH, NA_WIDTH, NA_WIDTH, GLA_KW, GLA_KW, GLA_VW, GLA_VW, GLA_GATE_RANK, GLA_GATE_RANK)
IN_AB = 3 * NA_WIDTH + 2 * GLA_KW + 2 * GLA_VW + 2 * GLA_GATE_RANK
SWA_HEADS = 16
SWA_KV_HEADS = 4
SWA_GROUP = SWA_HEADS // SWA_KV_HEADS
SWA_WINDOW = 128
SWA_BLOCK = 128
IN_C = (SWA_HEADS + 2 * SWA_KV_HEADS) * HEAD_DIM
D_FF = 2816
CONV_W = 3
ROPE_BASE = 10000.0
ROPE_AXIS_DIM = HEAD_DIM // 2
EPS = 1e-6
NEG_INF = -1e30

kernel_name = 'hybrid_na_gla_swa_prefix_dit_trunk'

def rmsnorm(x, g):
    xf = x.astype(jnp.float32)
    y = xf * lax.rsqrt(jnp.mean(xf * xf, axis=-1, keepdims=True) + EPS)
    return (y * g.astype(jnp.float32)).astype(x.dtype)

def modulate(h, shift, scale):
    return h * (1 + scale) + shift

def axial_rope_tables(n):
    t = jnp.arange(n)
    row = (t // GRID_W).astype(jnp.float32)
    col = (t % GRID_W).astype(jnp.float32)
    inv = 1.0 / (ROPE_BASE ** (jnp.arange(0, ROPE_AXIS_DIM, 2, dtype=jnp.float32) / ROPE_AXIS_DIM))
    ang = jnp.concatenate([row[:, None] * inv, col[:, None] * inv], axis=-1)
    return jnp.cos(ang), jnp.sin(ang)

def apply_rope(x, cos, sin):
    shp = (1, cos.shape[0]) + (1,) * (x.ndim - 3) + (cos.shape[1],)
    cos, sin = cos.reshape(shp), sin.reshape(shp)
    x1, x2 = x[..., 0::2], x[..., 1::2]
    out = jnp.stack([x1 * cos - x2 * sin, x1 * sin + x2 * cos], axis=-1)
    return out.reshape(x.shape).astype(x.dtype)

def joint_softmax(parts, sink=None):
    m = functools.reduce(jnp.maximum, [jnp.max(s, axis=-1, keepdims=True) for s in parts])
    if sink is not None:
        m = jnp.maximum(m, sink)
    ps = [jnp.exp(s - m) for s in parts]
    den = functools.reduce(jnp.add, [jnp.sum(p, axis=-1, keepdims=True) for p in ps])
    if sink is not None:
        den = den + jnp.exp(sink - m)
    return [p / den for p in ps]

def context_attention(q, k, v):
    B, n, H, d = q.shape
    s = jnp.einsum('bqhd,bkhd->bhqk', q, k).astype(jnp.float32) * d ** -0.5
    p = jax.nn.softmax(s, axis=-1).astype(v.dtype)
    return jnp.einsum('bhqk,bkhd->bqhd', p, v).reshape(B, n, H * d)

def neighbourhood_attention(q, k, v, k_ctx, v_ctx, rpb):
    B, S, H, d = q.shape
    rows = S // GRID_W
    kh = min(NA_WIN_H_MAX, rows)
    r = jnp.arange(rows)
    r_start = jnp.clip(r - kh // 2, 0, rows - kh)
    row_idx = r_start[:, None] + jnp.arange(kh)[None, :]
    cidx = jnp.arange(GRID_W)
    c_start = jnp.clip(cidx - NA_WIN_W // 2, 0, GRID_W - NA_WIN_W)
    col_ok = (cidx[None, :] >= c_start[:, None]) & (cidx[None, :] < c_start[:, None] + NA_WIN_W)
    dr = row_idx - r[:, None] + (NA_WIN_H_MAX - 1)
    dc = jnp.clip(cidx[None, :] - cidx[:, None] + NA_WIN_W - 1, 0, 2 * NA_WIN_W - 2)
    bias = rpb[:, dr[:, None, :, None], dc[None, :, None, :]].astype(jnp.float32)
    bias = jnp.where(col_ok[None, None, :, None, :], bias, NEG_INF).reshape(H, rows, GRID_W, kh * GRID_W)
    qg = q.reshape(B, rows, GRID_W, H, d)
    kg = jnp.take(k.reshape(B, rows, GRID_W, H, d), row_idx, axis=1).reshape(B, rows, kh * GRID_W, H, d)
    vg = jnp.take(v.reshape(B, rows, GRID_W, H, d), row_idx, axis=1).reshape(B, rows, kh * GRID_W, H, d)
    scale = d ** -0.5
    s_lat = jnp.einsum('brqhd,brkhd->bhrqk', qg, kg).astype(jnp.float32) * scale + bias[None]
    s_ctx = jnp.einsum('brqhd,bchd->bhrqc', qg, k_ctx).astype(jnp.float32) * scale
    p_lat, p_ctx = joint_softmax([s_lat, s_ctx])
    o = (jnp.einsum('bhrqk,brkhd->brqhd', p_lat.astype(v.dtype), vg)
         + jnp.einsum('bhrqc,bchd->brqhd', p_ctx.astype(v.dtype), v_ctx))
    return o.reshape(B, S, H * d)

def gla_log_decay(z_low, w2, b):
    z = z_low.astype(jnp.float32) @ w2.astype(jnp.float32) + b.astype(jnp.float32)
    return jax.nn.log_sigmoid(z) / GLA_TAU

def gla_chunked(q, k, v, log_a, s0, with_output):
    B, T, H, dk = k.shape
    dv = v.shape[-1]
    n = T // GLA_CHUNK
    blk = lambda t: t.astype(jnp.float32).reshape(B, n, GLA_CHUNK, H, t.shape[-1])
    kc, vc = blk(k), blk(v)
    b = jnp.cumsum(blk(log_a), axis=2)
    b_last = b[:, :, -1:]
    d_state = jnp.einsum('bnchd,bnchv->bnhdv', kc * jnp.exp(b_last - b), vc)
    decay = jnp.exp(b_last[:, :, 0])

    def step(s, inp):
        dec, ds = inp
        return dec[..., None] * s + ds, (s if with_output else None)

    s_final, s_in = lax.scan(step, s0, (jnp.moveaxis(decay, 1, 0), jnp.moveaxis(d_state, 1, 0)))
    if not with_output:
        return None, s_final
    qt = blk(q) * jnp.exp(b)
    kt = kc * jnp.exp(-b)
    tri = jnp.tril(jnp.ones((GLA_CHUNK, GLA_CHUNK), dtype=bool))
    att = jnp.where(tri, jnp.einsum('bnqhd,bnkhd->bnhqk', qt, kt), 0.0)
    o = jnp.einsum('bnhqk,bnkhv->bnqhv', att, vc) + jnp.einsum('bnqhd,nbhdv->bnqhv', qt, s_in)
    return o.reshape(B, T, H, dv), s_final

def gla_output(o, r, g):
    B, T = o.shape[:2]
    on = (o * lax.rsqrt(jnp.mean(o * o, axis=-1, keepdims=True) + EPS)).reshape(B, T, GLA_VW)
    return on.astype(r.dtype) * g * jax.nn.silu(r)

def project_na_gla(h, w_in, wa2, ba):
    B, n, _ = h.shape
    cuts, acc = [], 0
    for size in AB_SIZES[:-1]:
        acc += size
        cuts.append(acc)
    qa, ka, va, qb, kb, vb, rb, z_fwd, z_bwd = jnp.split(h @ w_in, cuts, axis=-1)
    na = lambda t: t.reshape(B, n, NA_HEADS, HEAD_DIM)
    gk = lambda t: t.reshape(B, n, GLA_HEADS, GLA_DK)
    la = (gk(gla_log_decay(z_fwd, wa2[0], ba[0])), gk(gla_log_decay(z_bwd, wa2[1], ba[1])))
    return (na(qa), na(ka), na(va), gk(qb) * GLA_DK ** -0.5, gk(kb),
            vb.reshape(B, n, GLA_HEADS, GLA_DV), rb, la)

def mixer_na_gla(hc, hl, w_in, rpb, wa2, ba, g_out, need_ctx):
    qa_c, ka_c, va_c, qb_c, kb_c, vb_c, rb_c, la_c = project_na_gla(hc, w_in, wa2, ba)
    qa_l, ka_l, va_l, qb_l, kb_l, vb_l, rb_l, la_l = project_na_gla(hl, w_in, wa2, ba)
    flip = lambda t: jnp.flip(t, axis=1)
    zero = jnp.zeros((hl.shape[0], GLA_HEADS, GLA_DK, GLA_DV), jnp.float32)
    o_cf, s_cf = gla_chunked(qb_c, kb_c, vb_c, la_c[0], zero, need_ctx)
    o_cb, s_cb = gla_chunked(flip(qb_c), flip(kb_c), flip(vb_c), flip(la_c[1]), zero, need_ctx)
    o_lf, _ = gla_chunked(qb_l, kb_l, vb_l, la_l[0], s_cf, True)
    o_lb, _ = gla_chunked(flip(qb_l), flip(kb_l), flip(vb_l), flip(la_l[1]), s_cb, True)
    y_l = jnp.concatenate([neighbourhood_attention(qa_l, ka_l, va_l, ka_c, va_c, rpb),
                           gla_output(o_lf + flip(o_lb), rb_l, g_out)], axis=-1)
    y_c = None
    if need_ctx:
        y_c = jnp.concatenate([context_attention(qa_c, ka_c, va_c),
                               gla_output(o_cf + flip(o_cb), rb_c, g_out)], axis=-1)
    return y_c, y_l

def mixer_swa(hc, hl, w_in, sink, cos, sin, need_ctx):
    B, T, _ = hl.shape
    KV, G, d = SWA_KV_HEADS, SWA_GROUP, HEAD_DIM
    cut_q, cut_k = SWA_HEADS * d, (SWA_HEADS + KV) * d

    def proj(h):
        n = h.shape[1]
        q, k, v = jnp.split(h @ w_in, [cut_q, cut_k], axis=-1)
        return q.reshape(B, n, KV, G, d), k.reshape(B, n, KV, d), v.reshape(B, n, KV, d)

    qc, kc, vc = proj(hc)
    ql, kl, vl = proj(hl)
    ql, kl = apply_rope(ql, cos, sin), apply_rope(kl, cos, sin)
    scale = d ** -0.5
    sink_f = sink.astype(jnp.float32).reshape(KV, G)
    nb = T // SWA_BLOCK
    qb = ql.reshape(B, nb, SWA_BLOCK, KV, G, d)

    def band(t):
        tp = jnp.pad(t.reshape(B, nb, SWA_BLOCK, KV, d), ((0, 0), (1, 1), (0, 0), (0, 0), (0, 0)))
        return jnp.concatenate([tp[:, :-2], tp[:, 1:-1], tp[:, 2:]], axis=2)

    kb, vb = band(kl), band(vl)
    qpos = jnp.arange(T).reshape(nb, SWA_BLOCK)
    kpos = jnp.arange(nb)[:, None] * SWA_BLOCK + jnp.arange(-SWA_BLOCK, 2 * SWA_BLOCK)[None, :]
    ok = ((jnp.abs(qpos[:, :, None] - kpos[:, None, :]) <= SWA_WINDOW)
          & (kpos[:, None, :] >= 0) & (kpos[:, None, :] < T))
    s_lat = jnp.einsum('bnqhgd,bnmhd->bhgnqm', qb, kb).astype(jnp.float32) * scale
    s_lat = jnp.where(ok[None, None, None], s_lat, NEG_INF)
    s_ctx = jnp.einsum('bnqhgd,bchd->bhgnqc', qb, kc).astype(jnp.float32) * scale
    p_lat, p_ctx = joint_softmax([s_lat, s_ctx], sink_f[None, :, :, None, None, None])
    o = (jnp.einsum('bhgnqm,bnmhd->bnqhgd', p_lat.astype(vb.dtype), vb)
         + jnp.einsum('bhgnqc,bchd->bnqhgd', p_ctx.astype(vc.dtype), vc))
    y_l = o.reshape(B, T, SWA_HEADS * d)
    y_c = None
    if need_ctx:
        s_cc = jnp.einsum('bqhgd,bchd->bhgqc', qc, kc).astype(jnp.float32) * scale
        (p_cc,) = joint_softmax([s_cc], sink_f[None, :, :, None, None])
        y_c = jnp.einsum('bhgqc,bchd->bqhgd', p_cc.astype(vc.dtype), vc).reshape(B, hc.shape[1], SWA_HEADS * d)
    return y_c, y_l

def conv_ffn(h, w_up, conv_w, conv_b, w_down):
    u = h @ w_up
    T = u.shape[1]
    pad = CONV_W // 2
    up = jnp.pad(u, ((0, 0), (pad, pad), (0, 0)))
    u = functools.reduce(jnp.add, [up[:, t:t + T] * conv_w[t] for t in range(CONV_W)]) + conv_b
    gate, val = jnp.split(u, 2, axis=-1)
    return (jax.nn.silu(gate) * val) @ w_down

def setup_inputs(seed: int = 0) -> dict:
    key = jax.random.key(seed)
    ks = iter(jax.random.split(key, 32))
    f32 = jnp.float32
    D = D_MODEL

    def w(shape, fan_in, s=1.0):
        return jax.random.normal(next(ks), shape, f32) * (s * fan_in ** -0.5)

    def gain(shape):
        return 1.0 + 0.1 * jax.random.normal(next(ks), shape, f32)

    def small(shape, s=0.02):
        return s * jax.random.normal(next(ks), shape, f32)

    return {
        'x': jax.random.normal(next(ks), (BATCH, SEQ, D), f32),
        'c': jax.random.normal(next(ks), (BATCH, D), f32),
        'ctx': jax.random.normal(next(ks), (BATCH, CTX_LEN, D), f32),
        'c_ctx': jax.random.normal(next(ks), (D,), f32),
        'w_mod': w((DEPTH, D, 6 * D), D, 0.5),
        'b_mod': small((DEPTH, 6 * D)),
        'g_mix_pre': gain((DEPTH, D)),
        'g_mix_post': gain((DEPTH, D)),
        'g_ffn_pre': gain((DEPTH, D)),
        'g_ffn_post': gain((DEPTH, D)),
        'w_out': w((DEPTH, D, D), D),
        'w_up': w((DEPTH, D, 2 * D_FF), D),
        'conv_w': w((DEPTH, CONV_W, 2 * D_FF), CONV_W),
        'conv_b': small((DEPTH, 2 * D_FF)),
        'w_down': w((DEPTH, D_FF, D), D_FF),
        'w_in_ab': w((N_EVEN, D, IN_AB), D),
        'na_rpb': small((N_EVEN, NA_HEADS, 2 * NA_WIN_H_MAX - 1, 2 * NA_WIN_W - 1), 0.1),
        'gla_wa2': w((N_EVEN, 2, GLA_GATE_RANK, GLA_KW), GLA_GATE_RANK),
        'gla_ba': small((N_EVEN, 2, GLA_KW), 0.1),
        'gla_g': gain((N_EVEN, GLA_VW)),
        'w_in_c': w((N_ODD, D, IN_C), D),
        'swa_sink': jax.random.normal(next(ks), (N_ODD, SWA_HEADS), f32),
    }

def reference(x, c, ctx, c_ctx, w_mod, b_mod, g_mix_pre, g_mix_post, g_ffn_pre, g_ffn_post,
              w_out, w_up, conv_w, conv_b, w_down, w_in_ab, na_rpb, gla_wa2, gla_ba, gla_g,
              w_in_c, swa_sink):
    xl, xc = x, ctx
    cos, sin = axial_rope_tables(x.shape[1])
    s_lat = jax.nn.silu(c)
    s_ctx = jax.nn.silu(c_ctx)
    for i in range(DEPTH):
        need_ctx = i < DEPTH - 1
        j = i // 2
        m_l = jnp.split((s_lat @ w_mod[i] + b_mod[i])[:, None, :], 6, axis=-1)
        m_c = jnp.split(s_ctx @ w_mod[i] + b_mod[i], 6, axis=-1)
        hl = modulate(rmsnorm(xl, g_mix_pre[i]), m_l[0], m_l[1])
        hc = modulate(rmsnorm(xc, g_mix_pre[i]), m_c[0], m_c[1])
        if i % 2 == 0:
            yc, yl = mixer_na_gla(hc, hl, w_in_ab[j], na_rpb[j], gla_wa2[j], gla_ba[j], gla_g[j], need_ctx)
        else:
            yc, yl = mixer_swa(hc, hl, w_in_c[j], swa_sink[j], cos, sin, need_ctx)
        xl = xl + m_l[2] * rmsnorm(yl @ w_out[i], g_mix_post[i])
        hl = modulate(rmsnorm(xl, g_ffn_pre[i]), m_l[3], m_l[4])
        xl = xl + m_l[5] * rmsnorm(conv_ffn(hl, w_up[i], conv_w[i], conv_b[i], w_down[i]), g_ffn_post[i])
        if need_ctx:
            xc = xc + m_c[2] * rmsnorm(yc @ w_out[i], g_mix_post[i])
            hc = modulate(rmsnorm(xc, g_ffn_pre[i]), m_c[3], m_c[4])
            xc = xc + m_c[5] * rmsnorm(conv_ffn(hc, w_up[i], conv_w[i], conv_b[i], w_down[i]), g_ffn_post[i])
    return xl


_drawn_inputs = setup_inputs


def setup_inputs(seed=0):
    import zlib

    import numpy as np

    out = dict(_drawn_inputs(seed))
    spreads = {}
    factors = {'conv_b': 5.324, 'na_rpb': 8.0, 'gla_ba': 4.537, 'swa_sink': 8.0}
    for name, (base, spread) in spreads.items():
        noise = np.random.default_rng([zlib.crc32(name.encode()), seed]).standard_normal(out[name].shape)
        drawn = base * np.exp(spread * noise) if base else spread * noise
        out[name] = jnp.asarray(drawn.astype(out[name].dtype))
    for name, factor in factors.items():
        out[name] = (out[name] * factor).astype(out[name].dtype)
    return out
```

```python
from contextlib import ExitStack

import concourse.bass as bass
from concourse import mybir
from concourse.alu_op_type import AluOpType as ALU

ACT = mybir.ActivationFunctionType
AX_X = mybir.AxisListType.X
F32 = mybir.dt.float32
F32R = mybir.dt.float32r
ds = bass.ds

P = 128
D = 1024
KD = D // P
LAT, CTXN = 1024, 256
TOK = LAT + CTXN
LAT_TILES, CTX_TILES = LAT // P, CTXN // P
GRID_W = 64
HEAD = 64
DEPTH = 2
NA_HEADS, NA_ROWS, NA_WIN = 8, 8, 16
NAW = NA_HEADS * HEAD
GLA_HEADS, DK, DV, CHUNK, RANK = 4, 64, 128, 64, 16
KW, VW = GLA_HEADS * DK, GLA_HEADS * DV
IN_AB = 3 * NAW + 2 * KW + 2 * VW + 2 * RANK
SWA_HEADS, KV, GROUP = 16, 4, 4
IN_C = (SWA_HEADS + 2 * KV) * HEAD
DFF = 2816
FT = DFF // P
TAU = 16.0
EPS = 1e-6
NEG = -1e30
SCALE = HEAD ** -0.5

PARAM_ROWS = [("c", KD), ("c_ctx", KD), ("b_mod", DEPTH * 6 * KD), ("g_mix_pre", DEPTH * KD), ("g_mix_post", DEPTH * KD),
              ("g_ffn_pre", DEPTH * KD), ("g_ffn_post", DEPTH * KD), ("conv_w", DEPTH * 3 * 2 * FT),
              ("conv_b", DEPTH * 2 * FT), ("gla_ba", 2 * KW // P), ("gla_g", VW // P)]
PCOL, _at = {}, 0
for _name, _count in PARAM_ROWS:
    PCOL[_name] = _at
    _at += _count
N_PCOL = _at
P_TILES = -(-N_PCOL // P)

CONST_COLS = [("ident", P), ("flip", P), ("tri_f", P), ("tri_b", P), ("na_ok", GRID_W), ("na_neg", GRID_W),
              ("swa_mask", 3 * P)]
CCOL, _at = {}, 0
for _name, _count in CONST_COLS:
    CCOL[_name] = _at
    _at += _count
N_CONST = _at

EDGE_SLOTS, INNER_SLOTS = 15, 9
BIAS_COLS = (EDGE_SLOTS + INNER_SLOTS) * GRID_W


class Net:

    def __init__(self, ins, scratch):
        self.x, self.c, self.ctx, self.c_ctx, self.w_mod, self.b_mod = (
            ins[n] for n in ("x", "c", "ctx", "c_ctx", "w_mod", "b_mod"))
        self.g_mix_pre, self.g_mix_post, self.g_ffn_pre, self.g_ffn_post, self.w_out, self.w_up = (
            ins[n] for n in ("g_mix_pre", "g_mix_post", "g_ffn_pre", "g_ffn_post", "w_out", "w_up"))
        self.conv_w, self.conv_b, self.w_down, self.w_in_ab, self.na_rpb, self.gla_wa2 = (
            ins[n] for n in ("conv_w", "conv_b", "w_down", "w_in_ab", "na_rpb", "gla_wa2"))
        self.gla_ba, self.gla_g, self.w_in_c, self.swa_sink, self.const_d, self.rope_d = (
            ins[n] for n in ("gla_ba", "gla_g", "w_in_c", "swa_sink", "const_d", "rope_d"))
        self.proj0_d, self.y0_d, self.x1_d, self.hid0_d, self.x2_d, self.proj1_d = (
            scratch[n] for n in ("proj0", "y0", "x1", "hid0", "x2", "proj1"))
        self.y1_d, self.x3_d, self.hid1_d, self.bias_d, self.rpb_rows_d, self.mod_d = (
            scratch[n] for n in ("y1", "x3", "hid1", "bias", "rpb_rows", "mod"))


def sbuf(nc, ctx):
    return lambda name, shape, dt=F32: ctx.enter_context(nc.sbuf_tensor(name, shape, dt))


def psum(nc, ctx):
    return lambda name, shape: ctx.enter_context(nc.psum_tensor(name, shape, F32))


def sems(nc, net, ctx, stage):
    net.last_stage, net.this_stage = net.this_stage, []

    def make(name):
        s = ctx.enter_context(nc.semaphore(f"{stage}_{name}"))
        net.this_stage.append(s.num)
        return s
    return make


def clear_last_stage(pool, net):
    numbers = sorted(net.last_stage)
    while numbers:
        n = 1
        while n < len(numbers) and numbers[n] == numbers[0] + n:
            n += 1
        pool.sem_clear(range(numbers[0], numbers[0] + n))
        numbers = numbers[n:]


def param(net, name, first, count):
    return net.pcol[:, PCOL[name] + first:PCOL[name] + first + count]


def param_runs(net):
    src = {
        "c": net.c.rearrange("b (r p) -> (b r) p", p=P), "c_ctx": net.c_ctx.rearrange("(r p) -> r p", p=P),
        "b_mod": net.b_mod.rearrange("l (r p) -> (l r) p", p=P),
        "g_mix_pre": net.g_mix_pre.rearrange("l (r p) -> (l r) p", p=P),
        "g_mix_post": net.g_mix_post.rearrange("l (r p) -> (l r) p", p=P),
        "g_ffn_pre": net.g_ffn_pre.rearrange("l (r p) -> (l r) p", p=P),
        "g_ffn_post": net.g_ffn_post.rearrange("l (r p) -> (l r) p", p=P),
        "conv_w": net.conv_w.rearrange("l t (r p) -> (l t r) p", p=P),
        "conv_b": net.conv_b.rearrange("l (r p) -> (l r) p", p=P),
        "gla_ba": net.gla_ba.rearrange("n z (r p) -> (n z r) p", p=P),
        "gla_g": net.gla_g.rearrange("n (r p) -> (n r) p", p=P),
    }
    for name, count in PARAM_ROWS:
        done = 0
        while done < count:
            at = PCOL[name] + done
            n = min(count - done, P - at % P)
            yield at // P, at % P, n, src[name][done:done + n]
            done += n


def setup_stage(nc, net):
    SLOTS = 4
    CHUNKS = 6 * D // 512
    MROWS = 2 * 6 * KD
    with ExitStack() as ctx:
        sb, pb, sem = sbuf(nc, ctx), psum(nc, ctx), sems(nc, net, ctx, "setup")
        rows = sb("param_rows", [P, P_TILES, P])
        cond = sb("cond", [P, KD, 2])
        wm = [sb(f"w_mod{r}", [P, KD, 512]) for r in range(SLOTS)]
        mod_row = sb("mod_row", [2, DEPTH, 6 * D])
        mod_rows = sb("mod_rows", [MROWS, DEPTH, P])
        mod = sb("mod", [P, DEPTH, 6 * KD, 2])
        ps_cols = pb("ps_cols", [P, P_TILES, P])
        ps_mod = [pb(f"ps_mod{r}", [P, 512]) for r in range(2)]
        BR = NA_HEADS * EDGE_SLOTS
        pad = sb("rpb_pad", [BR, P])
        slid = sb("rpb_slid", [GRID_W, BR, GRID_W])
        table = sb("rpb_table", [P, BR, GRID_W])
        never = sb("never", [P, NA_HEADS, GRID_W])
        ps_b = [pb(f"ps_b{r}", [P, 512]) for r in range(2)]
        pad_set, b_mm, b_done = sem("pad_set"), sem("b_mm"), sem("b_done")
        pad_in, pad_out, slid_in, b_stored = net.pad_in, net.pad_out, net.slid_in, net.b_stored
        B_STEPS = BR * GRID_W // 512
        const_in, rows_in = sem("const_in"), sem("rows_in")
        w_in = [sem(f"w_in{r}") for r in range(SLOTS)]
        row_out = [sem(f"row_out{n}") for n in range(DEPTH)]
        rows_back, mod_t = sem("rows_back"), sem("mod_t")
        cols_t, cols_done, cond_done = sem("cols_t"), sem("cols_done"), sem("cond_done")
        chunk_done, chunk_out, derived, half_set = (sem(n) for n in ("chunk_done", "chunk_out", "derived", "half_set"))
        runs = list(param_runs(net))
        with nc.Block() as block:
            @block.sync
            def _(sp):
                sp.dma_start(net.const[:], net.const_d).then_inc(const_in, 16)
                for tile, part, n, src in runs:
                    sp.dma_start(rows[part:part + n, tile, :], src).then_inc(rows_in, 16)
                for layer in range(DEPTH):
                    w = net.w_mod[layer].rearrange("(k p) n -> p k n", p=P)
                    with sp.Fori(0, CHUNKS // SLOTS) as i:
                        for r in range(SLOTS):
                            sp.wait_ge(chunk_done, i * SLOTS + (layer * CHUNKS + r + 1))
                            sp.dma_start(wm[r][:], w[:, :, ds(i * (SLOTS * 512) + r * 512, 512)]).then_inc(w_in[r], 16)
                for layer in range(DEPTH):
                    sp.wait_ge(chunk_out, 2 + (layer + 1) * CHUNKS)
                    sp.dma_start(net.mod_d[layer], mod_row[:, layer, :]).then_inc(row_out[layer], 16)
                for layer in range(DEPTH):
                    sp.wait_ge(row_out[layer], 16)
                    sp.dma_start(mod_rows[:, layer, :], net.mod_d[layer].rearrange("s (j p) -> (s j) p", p=P)).then_inc(rows_back, 16)

            @block.tensor
            def _(pe):
                pe.sem_inc(chunk_done, SLOTS)
                pe.wait_ge(const_in, 16)
                pe.wait_ge(rows_in, 16 * len(runs))
                for i in range(P_TILES):
                    n = min(P, N_PCOL - i * P)
                    t = pe.transpose(ps_cols[:, i, 0:n], rows[0:n, i, :], net.ident[0:n, 0:n])
                t.then_inc(cols_t, 1)
                pe.wait_ge(cond_done, 1)
                for layer in range(DEPTH):
                    with pe.Fori(0, CHUNKS // SLOTS) as i:
                        for r in range(SLOTS):
                            pe.wait_ge(w_in[r], i * 16 + 16 * (layer * CHUNKS // SLOTS + 1))
                            pe.wait_ge(chunk_out, i * SLOTS + (layer * CHUNKS + r + 1))
                            for k in range(KD):
                                m = pe.matmul(ps_mod[r % 2][0:2, :], cond[:, k, :], wm[r][:, k, :], start=(k == 0), stop=(k == KD - 1))
                            m.then_inc(chunk_done, 1)
                    if layer == 0:
                        pe.wait_ge(slid_in, 16)
                        flat = slid[:].rearrange("p r c -> p (r c)")
                        for n in range(B_STEPS):
                            if n >= 2:
                                pe.wait_ge(b_done, 2 * (n - 1))
                            pe.matmul(ps_b[n % 2][:], net.const[0:GRID_W, CCOL["flip"]:CCOL["flip"] + P],
                                      flat[:, n * 512:(n + 1) * 512], start=True, stop=True).then_inc(b_mm, 1)

                pe.wait_ge(rows_back, 16 * DEPTH)
                for layer in range(DEPTH):
                    m = pe.transpose(ps_mod[0][:, layer * P:layer * P + MROWS], mod_rows[:, layer, :], net.ident[0:MROWS, 0:MROWS])
                m.then_inc(mod_t, 1)

            @block.gpsimd
            def _(pool):
                clear_last_stage(pool, net)
                pool.memset(net.half[:], -0.5).then_inc(half_set, 1)
                pool.memset(never[:], 8 * NEG).then_inc(half_set, 1)
                pool.memset(pad[:], 0.0).then_inc(pad_set, 1)
                pool.wait_ge(pad_set, 1)
                width = 2 * NA_WIN - 1
                at = GRID_W - NA_WIN
                pool.dma_start(pad[:, at:at + width], net.na_rpb[0].rearrange("h r c -> (h r) c")).then_inc(pad_in, 16)
                pool.wait_ge(pad_in, 16)
                pool.dma_start(net.rpb_rows_d[0:BR, :], pad[:]).then_inc(pad_out, 16)
                pool.wait_ge(pad_out, 16)
                rows_d = net.rpb_rows_d
                slide = bass.AP(tensor=rows_d.tensor, offset=rows_d.offset, ap=[[1, GRID_W], [P, BR], [1, GRID_W]])
                pool.dma_start(slid[:], slide).then_inc(slid_in, 16)
                pool.wait_ge(b_done, 2 * B_STEPS)
                pool.wait_ge(half_set, 2)
                W, H = GRID_W, P // 2
                t4 = table[:].rearrange("p (h r) c -> p h (r c)", h=NA_HEADS)
                dst = net.bias_d.rearrange("h p n -> p h n")
                inner = EDGE_SLOTS * W
                pieces = [(dst[0:H, :, 0:15 * W], t4[0:H]), (dst[H:P, :, W:15 * W], t4[H:P, :, 0:14 * W]),
                          (dst[H:P, :, 0:W], never[H:P]),
                          (dst[0:H, :, inner:inner + 8 * W], t4[0:H, :, 3 * W:11 * W]),
                          (dst[0:H, :, inner + 8 * W:inner + 9 * W], never[0:H]),
                          (dst[H:P, :, inner + W:inner + 9 * W], t4[H:P, :, 3 * W:11 * W]),
                          (dst[H:P, :, inner:inner + W], never[H:P])]
                for to, what in pieces:
                    pool.dma_start(to, what).then_inc(b_stored, 16)
                pool.wait_ge(b_stored, 16 * len(pieces))

            @block.scalar
            def _(act):
                act.wait_ge(cols_done, 1)
                act.activation(cond[:], param(net, "c", 0, 2 * KD).rearrange("p (s k) -> p k s", s=2), ACT.Silu).then_inc(cond_done, 1)

            @block.vector
            def _(dve):
                dve.sem_inc(chunk_out, 2)
                dve.wait_ge(cols_t, 1)
                dve.tensor_copy(net.pcol[:], ps_cols[:].rearrange("p i n -> p (i n)")[:, 0:N_PCOL]).then_inc(cols_done, 1)
                for layer in range(DEPTH):
                    with dve.Fori(0, CHUNKS // SLOTS) as i:
                        for r in range(SLOTS):
                            dve.wait_ge(chunk_done, i * SLOTS + (layer * CHUNKS + r + 1 + SLOTS))
                            dst = mod_row[:, layer, ds(i * (SLOTS * 512) + r * 512, 512)]
                            dve.tensor_scalar(dst, ps_mod[r % 2][0:2, :], 1.0, None, ALU.mult).then_inc(chunk_out, 1)
                    if layer == 0:
                        ok, neg = (net.const[:, CCOL[n]:CCOL[n] + GRID_W].unsqueeze(1).to_broadcast([P, 8, GRID_W])
                                   for n in ("na_ok", "na_neg"))
                        for n in range(B_STEPS):
                            dst = table[:, 8 * n:8 * n + 8, :]
                            dve.wait_ge(b_mm, n + 1)
                            dve.scalar_tensor_tensor(dst, ps_b[n % 2][:].rearrange("p (r c) -> p r c", r=8), 1.0 / SCALE, ok,
                                                     ALU.mult, ALU.mult).then_inc(b_done, 1)
                            dve.wait_ge(b_done, 2 * n + 1)
                            dve.tensor_tensor(dst, dst, neg, ALU.add).then_inc(b_done, 1)
                bias = param(net, "b_mod", 0, DEPTH * 6 * KD).rearrange("p (l j o) -> p l j o", l=DEPTH, o=1)
                vectors = ps_mod[0][:].rearrange("p (l n) -> p l n", n=P)[:, 0:DEPTH, 0:MROWS].rearrange("p l (s j) -> p l j s", s=2)
                dve.wait_ge(mod_t, 1)
                dve.tensor_tensor(mod[:], vectors, bias.to_broadcast([P, DEPTH, 6 * KD, 2]), ALU.add).then_inc(derived, 1)
                dve.wait_ge(derived, 1)
                for layer in range(DEPTH):
                    for site, (pre, post) in enumerate((("g_mix_pre", "g_mix_post"), ("g_ffn_pre", "g_ffn_post"))):
                        part = [mod[:, layer, (3 * site + n) * KD:(3 * site + n + 1) * KD, :] for n in range(3)]
                        gain = [param(net, g, layer * KD, KD).unsqueeze(2).to_broadcast([P, KD, 2]) for g in (pre, post)]
                        dve.tensor_copy(net.shift[:, layer, site], part[0]).then_inc(derived, 1)
                        dve.scalar_tensor_tensor(net.scale[:, layer, site], part[1], 1.0, gain[0], ALU.add, ALU.mult).then_inc(derived, 1)
                        dve.tensor_tensor(net.gate[:, layer, site], part[2], gain[1], ALU.mult).then_inc(derived, 1)
                    taps = param(net, "conv_w", layer * 3 * 2 * FT, 3 * 2 * FT).rearrange("p (t f) -> p f t", t=3)
                    dve.tensor_copy(net.conv[:, layer, :, 0:3], taps).then_inc(derived, 1)
                    dve.tensor_copy(net.conv[:, layer, :, 3], param(net, "conv_b", layer * 2 * FT, 2 * FT)).then_inc(derived, 1)
                dve.wait_ge(derived, 1 + DEPTH * 8)


def project_stage(nc, net, name, layer, site, tiles, weights, out_T, kind, pairs, tail=None):
    NT = len(tiles)
    T = NT * P
    segs = [(s, min(s + 512, T)) for s in range(0, T, 512)]
    units = [(g, c) for g in range(len(segs)) for c in range(KD)]
    streams = [(0, LAT, 0)] + ([(LAT, T, 1)] if T > LAT else [])
    w_view = weights.rearrange("(k p) n -> p k n", p=P)
    bodies, odd = divmod(pairs, 2)
    assert odd == 0
    HI, LO = "hi", "lo"
    with ExitStack() as ctx:
        sb, pb, sem = sbuf(nc, ctx), psum(nc, ctx), sems(nc, net, ctx, name)
        h_hi, h_lo = (sb(f"{name}_h_{x}", [P, KD, T], F32R) for x in (HI, LO))
        raw = [sb(f"{name}_w_raw{s}", [P, KD, 2 * P]) for s in range(2)]
        w_hi, w_lo = ([sb(f"{name}_w_{x}{s}", [P, KD, 2 * P], F32R) for s in range(2)] for x in (HI, LO))
        region = sb(f"{name}_region", [P, 8 * TOK])
        xt = region[:, 0:NT * D].rearrange("p (t d) -> p t d", t=NT)
        buf = [region[:, n * TOK:n * TOK + T] for n in range(8)]
        hf = [sb(f"{name}_hf{s}", [P, 512]) for s in range(2)]
        stat = sb(f"{name}_stat", [P, 3, NT])
        tap = [sb(f"{name}_tap{s}", [P, 2, 4]) for s in range(2)]
        ps = [pb(f"{name}_ps{r}", [P, 3 * 512]) for r in range(2)]
        ps_t = [pb(f"{name}_ps_t{r}", [P, 512]) for r in range(2)]
        x_in = [sem(f"x_in{g}") for g in range(len(segs))]
        w_in = [sem(f"w_in{s}") for s in range(2)]
        sq, ms, rstd, hn, tr, mod1, h_ready = (sem(n) for n in ("sq", "ms", "rstd", "hn", "tr", "mod1", "h_ready"))
        whi, wlo, mm, conv1, act_gate, dve_step, out_ready, taps = (sem(n) for n in (
            "whi", "wlo", "mm", "conv1", "act_gate", "dve_step", "out_ready", "taps"))
        evac = [sem(f"evac{r}") for r in range(2)]
        stored = [sem(f"stored{n}") for n in range(2 if kind == "ffn" else 4)]
        STEPS = 4 * len(streams) + 1

        def cols(i, s):
            if kind == "ffn":
                return [(0, P, ds(i * (2 * P) + s * P, P)), (P, 2 * P, ds(i * (2 * P) + (s * P + DFF), P))]
            return [(0, 2 * P, ds(i * (4 * P) + s * 2 * P, 2 * P))]

        n_in = 32 if kind == "ffn" else 16

        with nc.Block() as block:
            @block.sync
            def _(sp):
                def load(i, s):
                    for a, b, src in cols(i, s):
                        sp.dma_start(raw[s][:, :, a:b], w_view[:, :, src]).then_inc(w_in[s], 16)

                def store(i, s):
                    if kind == "ffn":
                        sp.wait_ge(out_ready, i * 2 + s + 1)
                        sp.dma_start(out_T[ds(i * (2 * P) + s * P, P), 0:T], buf[4 + s]).then_inc(stored[s], 16)
                    else:
                        for r in range(2):
                            sp.wait_ge(evac[r], i * 2 + (s + 2))
                            sp.dma_start(out_T[ds(i * (4 * P) + (2 * s + r) * P, P), 0:T], buf[2 * s + r]).then_inc(stored[2 * s + r], 16)

                for done in stored:
                    sp.sem_inc(done, 16)
                for t in range(NT):
                    sp.dma_start(xt[:, t, :], tiles[t]).then_inc(x_in[t // 4], 16)
                    if t == 3:
                        for s in range(2):
                            load(0, s)
                with sp.Fori(0, bodies - 1) as b:
                    for s in range(2):
                        sp.wait_ge(wlo, b * 2 + (s + 1))
                        load(b + 1, s)
                        store(b, s)
                if tail:
                    sp.wait_ge(wlo, 2 * bodies - 1)
                    sp.dma_start(raw[0][:, :, 0:P], w_view[:, :, tail[0]:tail[0] + P]).then_inc(w_in[0], 16)
                for s in range(2):
                    store(bodies - 1, s)
                if tail:
                    sp.wait_ge(evac[0], 1 + pairs + 1)
                    rows = tail[0] + P - tail[1]
                    sp.dma_start(out_T[tail[1]:tail[1] + rows, 0:T], buf[0][P - rows:P, :]).then_inc(stored[0], 16)
                for n, done in enumerate(stored):
                    sp.wait_ge(done, 16 * (1 + bodies + (bool(tail) and n == 0)))

            @block.scalar
            def _(act):
                def squares(g):
                    own = range(4 * g, min(4 * g + 4, NT))
                    act.wait_ge(x_in[g], 16 * len(own))
                    for t in own:
                        if t:
                            act.wait_ge(sq, t)
                        act.activation(ps[0][:, 0:D], xt[:, t, :], ACT.Square, accum_out=stat[:, 0, t:t + 1]).then_inc(sq, 1)

                if kind == "plain":
                    act.sem_inc(evac[0], 1)
                for g in range(len(segs)):
                    squares(g)
                for u, (g, c) in enumerate(units):
                    a, b = segs[g]
                    stream = int(a >= LAT)
                    act.wait_ge(tr, u + 1)
                    if u >= 2:
                        act.wait_ge(h_ready, 2 * (u - 1))
                    act.activation(hf[u % 2][:, 0:b - a], ps_t[u % 2][:, 0:b - a], ACT.Identity,
                                   scale=net.scale[:, layer, site, c, stream:stream + 1],
                                   bias=net.shift[:, layer, site, c, stream:stream + 1]).then_inc(mod1, 1)

                def split(i, s, width=2 * P):
                    act.wait_ge(w_in[s], i * n_in + n_in)
                    act.wait_ge(mm, i * 4 + (2 * s + 2))
                    act.activation(w_hi[s][:, :, 0:width], raw[s][:, :, 0:width], ACT.Copy).then_inc(whi, 1)

                def evacuate(i, s):
                    if kind == "ffn":
                        act.wait_ge(taps, i * 2 + s + 1)
                        act.wait_ge(dve_step, i * (2 * STEPS) + ((s + 1) * STEPS))
                        for r in range(2):
                            act.wait_ge(mm, i * 4 + (2 * s + r + 5))
                            act.activation(buf[2 * s + r], ps[r][:, 0:T], ACT.Identity, scale=tap[s][:, r, 1:2],
                                           bias=tap[s][:, r, 3:4]).then_inc(conv1, 1)
                        act.wait_ge(dve_step, i * (2 * STEPS) + (2 * STEPS + s * STEPS + 2 * len(streams)))
                        act.activation(buf[6 + s], buf[2 * s], ACT.Silu).then_inc(act_gate, 1)
                    else:
                        act.wait_ge(mm, i * 4 + (2 * s + 5))
                        act.wait_ge(stored[2 * s], i * 16 + 16)
                        act.activation(buf[2 * s], ps[0][:, 0:T], ACT.Copy).then_inc(evac[0], 1)

                split(0, 0)
                with act.Fori(0, bodies - 1) as b:
                    split(b, 1)
                    evacuate(b, 0)
                    split(b + 1, 0)
                    evacuate(b, 1)
                split(bodies - 1, 1)
                evacuate(bodies - 1, 0)
                if tail:
                    act.wait_ge(w_in[0], 16 * (bodies + 1))
                    act.wait_ge(mm, 4 * bodies + 2)
                    act.activation(w_hi[0][:, :, 0:P], raw[0][:, :, 0:P], ACT.Copy).then_inc(whi, 1)
                evacuate(bodies - 1, 1)
                if tail:
                    act.wait_ge(mm, 4 + 2 * pairs + 1)
                    act.wait_ge(stored[0], 16 * (bodies + 1))
                    act.activation(buf[0], ps[0][:, 0:T], ACT.Copy).then_inc(evac[0], 1)

            @block.gpsimd
            def _(pool):
                clear_last_stage(pool, net)
                for g, (a, b) in enumerate(segs):
                    t0, t1 = a // P, b // P
                    pool.wait_ge(ms, g + 1)
                    pool.tensor_tensor(stat[:, 2, t0:t1], stat[:, 1, t0:t1], net.half[:, 0:t1 - t0], ALU.pow).then_inc(rstd, 1)

            @block.vector
            def _(dve):
                dve.sem_inc(dve_step, 2 * STEPS)
                for done in (evac if kind == "ffn" else evac[1:]):
                    dve.sem_inc(done, 1)
                for g, (a, b) in enumerate(segs):
                    t0, t1 = a // P, b // P
                    dve.wait_ge(sq, t1)
                    dve.tensor_scalar(stat[:, 1, t0:t1], stat[:, 0, t0:t1], 1.0 / D, EPS, ALU.mult, ALU.add).then_inc(ms, 1)
                    dve.wait_ge(rstd, g + 1)
                    for t in range(t0, t1):
                        dve.tensor_scalar(xt[:, t, :], xt[:, t, :], stat[:, 2, t:t + 1], None, ALU.mult).then_inc(hn, 1)
                for u, (g, c) in enumerate(units):
                    a, b = segs[g]
                    dve.wait_ge(mod1, u + 1)
                    dve.tensor_copy(h_hi[:, c, a:b], hf[u % 2][:, 0:b - a]).then_inc(h_ready, 1)
                    dve.wait_ge(h_ready, 2 * u + 1)
                    dve.tensor_tensor(h_lo[:, c, a:b], hf[u % 2][:, 0:b - a], h_hi[:, c, a:b].bitcast(F32), ALU.subtract)\
                       .then_inc(h_ready, 1)

                def split(i, s, width=2 * P):
                    dve.wait_ge(whi, i * 2 + s + 1)
                    dve.tensor_tensor(w_lo[s][:, :, 0:width], raw[s][:, :, 0:width], w_hi[s][:, :, 0:width].bitcast(F32),
                                      ALU.subtract).then_inc(wlo, 1)

                def evacuate(i, s):
                    if kind == "ffn":
                        base = 2 * STEPS + s * STEPS
                        step = 0
                        for r in range(2):
                            dve.wait_ge(conv1, i * 4 + (2 * s + r + 1))
                            for tapn, shift in ((0, -1), (2, 1)):
                                for lo, hi, _ in streams:
                                    dst = buf[2 * s + r][:, max(lo - shift, lo):min(hi - shift, hi)]
                                    src = ps[r][:, max(lo + shift, lo):min(hi + shift, hi)]
                                    last = tapn == 2 and hi == T
                                    o = dve.scalar_tensor_tensor(dst, src, tap[s][:, r, tapn:tapn + 1], dst, ALU.mult, ALU.add)
                                    o.then_inc(dve_step, 1)
                                    step += 1
                                    dve.wait_ge(dve_step, i * (2 * STEPS) + (base + step))
                            dve.sem_inc(evac[r], 1)
                        dve.wait_ge(act_gate, i * 2 + s + 1)
                        dve.wait_ge(stored[s], i * 16 + 16)
                        dve.tensor_tensor(buf[4 + s], buf[6 + s], buf[2 * s + 1], ALU.mult).then_inc(out_ready, 1)
                        dve.wait_ge(out_ready, i * 2 + s + 1)
                        dve.sem_inc(dve_step, 1)
                    else:
                        dve.wait_ge(mm, i * 4 + (2 * s + 6))
                        dve.wait_ge(stored[2 * s + 1], i * 16 + 16)
                        dve.tensor_copy(buf[2 * s + 1], ps[1][:, 0:T]).then_inc(evac[1], 1)

                def load_taps(i, s):
                    src = net.conv[:, layer].rearrange("p (r f) n -> p r f n", r=2)[:, :, ds(i * 2 + s, 1), :]
                    dve.tensor_scalar(tap[s][:].unsqueeze(2), src, 1.0, None, ALU.mult).then_inc(taps, 1)

                if kind == "ffn":
                    load_taps(0, 0)
                split(0, 0)
                with dve.Fori(0, bodies - 1) as b:
                    if kind == "ffn":
                        load_taps(b, 1)
                    split(b, 1)
                    evacuate(b, 0)
                    if kind == "ffn":
                        load_taps(b + 1, 0)
                    split(b + 1, 0)
                    evacuate(b, 1)
                if kind == "ffn":
                    load_taps(bodies - 1, 1)
                split(bodies - 1, 1)
                evacuate(bodies - 1, 0)
                if tail:
                    dve.wait_ge(whi, pairs + 1)
                    dve.tensor_tensor(w_lo[0][:, :, 0:P], raw[0][:, :, 0:P], w_hi[0][:, :, 0:P].bitcast(F32),
                                      ALU.subtract).then_inc(wlo, 1)
                evacuate(bodies - 1, 1)

            @block.tensor
            def _(pe):
                pe.sem_inc(mm, 4)
                for u, (g, c) in enumerate(units):
                    a, b = segs[g]
                    pe.wait_ge(hn, b // P)
                    if u >= 2:
                        pe.wait_ge(mod1, u - 1)
                    for t in range(a // P, b // P):
                        m = pe.transpose(ps_t[u % 2][:, t * P - a:t * P - a + P], xt[:, t, c * P:(c + 1) * P], net.ident)
                    m.then_inc(tr, 1)
                pe.wait_ge(h_ready, 2 * len(units))

                def product(s, r, width):
                    n = 0
                    for k in range(KD):
                        for w, h in ((w_hi, h_hi), (w_hi, h_lo), (w_lo, h_hi)):
                            for a, b in segs:
                                m = pe.matmul(ps[r][:, a:b], w[s][:, k, r * P:(r + 1) * P], h[:, k, a:b],
                                              start=(n == 0), stop=(n == 3 * KD - 1))
                            n += 1
                    m.then_inc(mm, 1)

                with pe.Fori(0, bodies) as b:
                    for s in range(2):
                        pe.wait_ge(wlo, b * 2 + s + 1)
                        for r in range(2):
                            pe.wait_ge(evac[r], b * 2 + (s + 1))
                            product(s, r, P)
                if tail:
                    pe.wait_ge(wlo, pairs + 1)
                    pe.wait_ge(evac[0], pairs + 1)
                    product(0, 0, P)


def close_stage(nc, net, name, layer, site, src_T, weights, width, x_tiles, out_tiles):
    NT = len(x_tiles)
    groups = [(g, min(g + 4, NT)) for g in range(0, NT, 4)]
    steps = width // (2 * P)
    w_view = weights.rearrange("(j k p) n -> j p k n", p=P, k=2)
    s_view = src_T.rearrange("(j k p) t -> j p k t", p=P, k=2)
    streams = 1 if NT == LAT_TILES else 2
    with ExitStack() as ctx:
        sb, pb, sem = sbuf(nc, ctx), psum(nc, ctx), sems(nc, net, ctx, name)
        w_raw = [sb(f"{name}_w_raw{s}", [P, 2, D]) for s in range(2)]
        w_hi, w_lo = ([sb(f"{name}_w_{x}{s}", [P, 2, D], F32R) for s in range(2)] for x in ("hi", "lo"))
        a_raw = [sb(f"{name}_a_raw{s}", [P, 2, 512]) for s in range(2)]
        a_hi, a_lo = ([sb(f"{name}_a_{x}{s}", [P, 2, 512], F32R) for s in range(2)] for x in ("hi", "lo"))
        gate = sb(f"{name}_gate", [P, 2, D])
        diag = [sb(f"{name}_diag{s}", [P, P]) for s in range(2)]
        ones = sb(f"{name}_ones", [P, P])
        xt = sb(f"{name}_xt", [P, 4, D])
        yt = sb(f"{name}_yt", [P, 2, D])
        sqb = sb(f"{name}_sqb", [P, D])
        stat = sb(f"{name}_stat", [P, 3, NT])
        ps = [pb(f"{name}_ps{m}", [P, D]) for m in range(4)]
        ld = [sem(f"ld{s}") for s in range(2)]
        (hi, lo, mm, y_done, read, ones_set, diag_set, gate_mm, gate_set, x_in, sq, ms, rstd, scaled,
         added) = (sem(n) for n in ("hi", "lo", "mm", "y_done", "read", "ones_set", "diag_set", "gate_mm", "gate_set",
                                     "x_in", "sq", "ms", "rstd", "scaled", "added"))
        stored = net.tile_stored
        base = net.tiles_stored * 16 // 2
        net.tiles_stored += NT
        diag_used = sem("diag_used")
        loops, rest = divmod(steps - 1, 2)

        def run_group(eng, g, step):
            J = g * steps
            step(J, 0, J % 2, True, steps == 1)
            whole = loops if rest else loops - 1
            if whole > 0:
                with eng.Fori(0, whole) as b:
                    for s in range(2):
                        step(J + 1 + s, b, (J + 1 + s) % 2, False, False)
            for j in range(1 + 2 * whole, steps):
                step(J + j, 0, (J + j) % 2, False, j == steps - 1)

        with nc.Block() as block:
            @block.sync
            def _(sp):
                for g, (t0, t1) in enumerate(groups):
                    def load(J, b, s, first, last):
                        sp.wait_ge(lo, b * 4 + (2 * J + 1 + 1))
                        sp.dma_start(w_raw[s][:], w_view[b * 2 + (J - g * steps)]).then_inc(ld[s], 16)
                        sp.dma_start(a_raw[s][:, :, 0:(t1 - t0) * P], s_view[b * 2 + (J - g * steps), :, :, t0 * P:t1 * P])\
                          .then_inc(ld[s], 16)
                        if first:
                            if g:
                                sp.wait_ge(added, t0)
                            for t in range(t0, t1):
                                sp.dma_start(xt[:, t - t0, :], x_tiles[t]).then_inc(x_in, 16)
                    run_group(sp, g, load)

            @block.gpsimd
            def _(pool):
                clear_last_stage(pool, net)
                pool.memset(ones[:], 1.0).then_inc(ones_set, 1)
                for t in range(NT):
                    pool.wait_ge(ms, t + 1)
                    pool.tensor_tensor(stat[:, 2, t:t + 1], stat[:, 1, t:t + 1], net.half[:, 0:1], ALU.pow).then_inc(rstd, 1)
                    if t >= 1:
                        pool.wait_ge(added, t)
                        pool.dma_start(out_tiles[t - 1], yt[:, (t - 1) % 2, :]).then_inc(stored[(t - 1) % 2], 16)
                pool.wait_ge(added, NT)
                pool.dma_start(out_tiles[NT - 1], yt[:, (NT - 1) % 2, :]).then_inc(stored[(NT - 1) % 2], 16)
                for s in range(2):
                    pool.wait_ge(stored[s], base + 16 * (NT // 2))

            @block.scalar
            def _(act):
                for s in range(streams):
                    act.wait_ge(gate_mm, s + 1)
                    act.activation(gate[:, s, :], ps[s][:], ACT.Copy).then_inc(gate_set, 1)
                for g, (t0, t1) in enumerate(groups):
                    n = (t1 - t0) * P

                    def split(J, b, s, first, last):
                        act.wait_ge(ld[s], b * 32 + 32 * (J // 2 + 1))
                        act.wait_ge(mm, b * 2 + J + 1)
                        act.activation(w_hi[s][:], w_raw[s][:], ACT.Copy).then_inc(hi, 1)
                        act.activation(a_hi[s][:, :, 0:n], a_raw[s][:, :, 0:n], ACT.Copy).then_inc(hi, 1)
                    run_group(act, g, split)
                    for t in range(t0, t1):
                        act.wait_ge(y_done, t + 1)
                        if t:
                            act.wait_ge(sq, t)
                        act.activation(sqb[:], ps[t - t0][:], ACT.Square, accum_out=stat[:, 0, t:t + 1]).then_inc(sq, 1)

            @block.vector
            def _(dve):
                dve.sem_inc(lo, 4)
                dve.wait_ge(ones_set, 1)
                for s in range(streams):
                    for c in range(KD):
                        n = s * KD + c
                        if n >= 2:
                            dve.wait_ge(diag_used, n - 1)
                        dve.tensor_scalar(diag[n % 2][:], net.ident, net.gate[:, layer, site, c, s:s + 1], None, ALU.mult)\
                           .then_inc(diag_set, 1)
                for g, (t0, t1) in enumerate(groups):
                    n = (t1 - t0) * P

                    def split(J, b, s, first, last):
                        dve.wait_ge(hi, b * 4 + (2 * J + 1))
                        dve.tensor_tensor(w_lo[s][:], w_raw[s][:], w_hi[s][:].bitcast(F32), ALU.subtract).then_inc(lo, 1)
                        dve.wait_ge(hi, b * 4 + (2 * J + 2))
                        dve.tensor_tensor(a_lo[s][:, :, 0:n], a_raw[s][:, :, 0:n], a_hi[s][:, :, 0:n].bitcast(F32),
                                          ALU.subtract).then_inc(lo, 1)
                    run_group(dve, g, split)
                    dve.wait_ge(gate_set, streams)
                    for t in range(t0, t1):
                        dve.wait_ge(sq, t + 1)
                        dve.tensor_scalar(stat[:, 1, t:t + 1], stat[:, 0, t:t + 1], 1.0 / D, EPS, ALU.mult, ALU.add).then_inc(ms, 1)
                        dve.wait_ge(rstd, t + 1)
                        if t >= 2:
                            dve.wait_ge(stored[t % 2], base + 16 * (t // 2))
                        dve.scalar_tensor_tensor(yt[:, t % 2, :], ps[t - t0][:], stat[:, 2, t:t + 1], gate[:, int(t >= LAT_TILES), :],
                                                 ALU.mult, ALU.mult).then_inc(scaled, 1)
                        dve.wait_ge(scaled, t + 1)
                        dve.wait_ge(x_in, 16 * t1)
                        dve.tensor_tensor(yt[:, t % 2, :], yt[:, t % 2, :], xt[:, t - t0, :], ALU.add).then_inc(added, 1)

            @block.tensor
            def _(pe):
                pe.sem_inc(mm, 2)
                for s in range(streams):
                    for c in range(KD):
                        n = s * KD + c
                        pe.wait_ge(diag_set, n + 1)
                        m = pe.matmul(ps[s][:, c * P:(c + 1) * P], ones[:], diag[n % 2][:], start=True, stop=True)
                        m.then_inc(diag_used, 1)
                    pe.wait_ge(diag_used, (s + 1) * KD)
                    pe.sem_inc(gate_mm, 1)
                pe.wait_ge(gate_set, streams)
                for g, (t0, t1) in enumerate(groups):
                    def multiply(J, b, s, first, last):
                        pe.wait_ge(lo, b * 4 + (2 * J + 2 + 4))
                        for m_ in range(t1 - t0):
                            if first and g:
                                pe.wait_ge(scaled, (t0 - 4) + m_ + 1)
                            for kk in range(2):
                                for n, (a, w) in enumerate(((a_hi, w_hi), (a_hi, w_lo), (a_lo, w_hi))):
                                    for half in range(2):
                                        m = pe.matmul(ps[m_][:, half * 512:(half + 1) * 512], a[s][:, kk, m_ * P:(m_ + 1) * P],
                                                      w[s][:, kk, half * 512:(half + 1) * 512],
                                                      start=(first and kk == 0 and n == 0), stop=(last and kk == 1 and n == 2))
                            if last:
                                m.then_inc(y_done, 1)
                        if last:
                            pe.wait_ge(y_done, t1)
                            pe.sem_inc(mm, 1)
                        else:
                            m.then_inc(mm, 1)
                    run_group(pe, g, multiply)


def attention_stage(nc, net, name, proj, y_T, banded):
    GROUPS = KV if banded else NA_HEADS // 2
    BODIES = GROUPS // 2
    CHUNKS = 2 if banded else 1
    T_OUT = LAT if banded else TOK
    HALF = P // 2
    with ExitStack() as ctx:
        sb, pb, sem = sbuf(nc, ctx), psum(nc, ctx), sems(nc, net, ctx, name)
        q = [sb(f"{name}_q{r}", [P, CHUNKS, T_OUT]) for r in range(2)]
        k = [sb(f"{name}_k{r}", [P, 2, TOK]) for r in range(2)]
        vt = [sb(f"{name}_vt{r}", [P, TOK]) for r in range(2)]
        v = [sb(f"{name}_v{r}", [P, TOK // P, P]) for r in range(2)]
        yt = [sb(f"{name}_yt{r}", [P, CHUNKS, T_OUT]) for r in range(2)]
        yb = [sb(f"{name}_yb{n}", [P, CHUNKS * P]) for n in range(2)]
        prob = [sb(f"{name}_prob{n}", [P, 832]) for n in range(2)]
        pt = [sb(f"{name}_pt{n}", [P, 7 * P]) for n in range(2)]
        mx = sb(f"{name}_mx", [P, 3, 2])
        den = sb(f"{name}_den", [P, 4, 3])
        if banded:
            q_sw = [sb(f"{name}_q_sw{r}", [P, CHUNKS, LAT]) for r in range(2)]
            k_sw = [sb(f"{name}_k_sw{r}", [P, LAT]) for r in range(2)]
            rope = sb(f"{name}_rope", [P, 2, LAT])
            sink_all = sb(f"{name}_sink_all", [P, SWA_HEADS])
            sink8 = [sb(f"{name}_sink8{r}", [P, GROUP]) for r in range(2)]
        else:
            bias = [sb(f"{name}_bias{r}", [P, 2, BIAS_COLS]) for r in range(2)]
        ps_s = [pb(f"{name}_ps_s{n}", [P, 1024]) for n in range(2)]
        ps_p = pb(f"{name}_ps_p", [P, 1024])
        ps_o = pb(f"{name}_ps_o", [P, 512])
        ps_y = pb(f"{name}_ps_y", [P, 512])
        ld = [sem(f"ld{r}") for r in range(2)]
        stored = [sem(f"stored{r}") for r in range(2)]
        held, turning, padded, v_padded = (sem(n) for n in ("held", "turning", "padded", "v_padded"))
        (scores, front, maxed, probs, trans, pt_a, pt_b, out_mm, recip, normed, y_tr, y_ev, v_tr, v_ev, zeroed,
         rotated, rope_in, sinks) = (sem(n) for n in (
             "scores", "front", "maxed", "probs", "trans", "pt_a", "pt_b", "out_mm", "recip", "normed", "y_tr", "y_ev",
             "v_tr", "v_ev", "zeroed", "rotated", "rope_in", "sinks"))

        def unit(r, tile, head):
            if banded:
                chunk, half, vcol = head // 2, head % 2, 0
            else:
                chunk, half, vcol = 0, head, head * HEAD
            u = {"r": r, "vcol": vcol, "q": q[r][:, chunk, tile * P:(tile + 1) * P], "head": head}
            if tile >= LAT_TILES:
                lat, u["bias"] = (0, 0), None
            elif banded:
                lat = (max(tile - 1, 0) * P, min(tile + 2, LAT_TILES) * P)
                c0 = CCOL["swa_mask"] + (P if tile == 0 else 0)
                u["bias"] = net.const[:, c0:c0 + lat[1] - lat[0]]
            else:
                first, second = (min(max(row - NA_ROWS // 2, 0), LAT // GRID_W - NA_ROWS) for row in (2 * tile, 2 * tile + 1))
                inner = first != second
                n = (NA_ROWS + 1) if inner else NA_ROWS
                lat = (first * GRID_W, (first + n) * GRID_W)
                slot = EDGE_SLOTS if inner else first - 2 * tile + NA_ROWS - 1
                u["bias"] = bias[r][:, head, slot * GRID_W:(slot + n) * GRID_W]
            keys, blocks = [], []
            at = 0
            for a, b in (lat, (LAT, TOK)):
                done = a
                while done < b:
                    n = min(b - done, 512 - at % 512)
                    keys.append((at, n, k[r][:, half, done:done + n]))
                    at, done = at + n, done + n
                for t in range(a, b, P):
                    n = min(P, b - t)
                    blocks.append((at - (b - a) + t - a, n, v[r][0:n, t // P, :]))
            u.update(keys=keys, blocks=blocks, n=at, lat=lat[1] - lat[0])
            return u

        heads = GROUP if banded else 2
        tiles = range(T_OUT // P)
        units = [unit(r, tile, head) for r in range(2) for tile in tiles for head in range(heads)]
        U = len(units)
        UG = U // 2
        Y = U // heads
        YG = Y // 2
        front_of = [0]
        for w in units:
            front_of.append(front_of[-1] + (2 if w["bias"] is not None else 1))
        F = front_of[-1]
        V_GROUPS = [(t, min(t + 4, TOK // P)) for t in range(0, TOK // P, 4)]
        VW_ = HEAD if banded else P
        N_LD = 10 if banded else 5
        SWITCH = UG - 1
        TURNED = (SWITCH - 3) // heads

        with nc.Block() as block:
            @block.sync
            def _(sp):
                def load(i, r):
                    g = i * 2 + r
                    inc = lambda d: d.then_inc(ld[r], 16)
                    if banded:
                        qr = proj[ds(i * (2 * GROUP * HEAD) + r * GROUP * HEAD, GROUP * HEAD), :]
                        kr = proj[ds(i * (2 * HEAD) + (SWA_HEADS + r) * HEAD, HEAD), :]
                        vr = proj[ds(i * (2 * HEAD) + (SWA_HEADS + KV + r) * HEAD, HEAD), :]
                        swap = qr.rearrange("(c h two) t -> two h c t", c=2, two=2)
                        kswap = kr.rearrange("(h two) t -> two h t", two=2)
                        inc(sp.dma_start(q[r][:], qr.rearrange("(c p) t -> p c t", c=2)[:, :, 0:LAT]))
                        for two in range(2):
                            inc(sp.dma_start(q_sw[r][two::2], swap[1 - two, :, :, 0:LAT]))
                        for half in range(2):
                            inc(sp.dma_start(k[r][half * HALF:(half + 1) * HALF, half, :], kr))
                            for two in range(2):
                                inc(sp.dma_start(k_sw[r][half * HALF + two:(half + 1) * HALF:2, :], kswap[1 - two, :, 0:LAT]))
                        inc(sp.dma_start(vt[r][0:HEAD, :], vr))
                    else:
                        for half in range(2):
                            kr = proj[ds(i * (2 * P) + r * P + NAW + half * HALF, HALF), :]
                            inc(sp.dma_start(k[r][half * HALF:(half + 1) * HALF, half, :], kr))
                        for dst, base in ((q[r][:, 0, :], 0), (vt[r][:], 2 * NAW)):
                            inc(sp.dma_start(dst, proj[ds(i * (2 * P) + r * P + base, P), :]))
                        inc(sp.dma_start(bias[r][:], net.bias_d[ds(i * 4 + 2 * r, 2)].rearrange("h p n -> p h n")))

                def store(i, r):
                    sp.wait_ge(y_ev, i * Y + ((r + 1) * YG + 1))
                    rows = y_T[ds(i * (2 * CHUNKS * P) + r * CHUNKS * P, CHUNKS * P), 0:T_OUT]
                    sp.dma_start(rows.rearrange("(c p) t -> p c t", c=CHUNKS), yt[r][:]).then_inc(stored[r], 16)

                for r in range(2):
                    sp.sem_inc(stored[r], 16)
                if banded:
                    sp.dma_start(rope[:], net.rope_d.rearrange("n p t -> p n t")).then_inc(rope_in, 16)
                    sp.dma_start(sink_all[:], net.swa_sink[0:1, :].to_broadcast([P, SWA_HEADS])).then_inc(rope_in, 16)
                for r in range(2):
                    load(0, r)
                with sp.Fori(0, BODIES - 1) as i:
                    for r in range(2):
                        store(i, r)
                        load(i + 1, r)
                for r in range(2):
                    store(BODIES - 1, r)
                for r in range(2):
                    sp.wait_ge(stored[r], 16 * (1 + BODIES))

            @block.gpsimd
            def _(pool):
                clear_last_stage(pool, net)
                for r in range(2):
                    for half in range(2):
                        pool.memset(k[r][(1 - half) * HALF:(2 - half) * HALF, half, :], 0.0).then_inc(padded, 1)
                if not banded:
                    return
                pool.wait_ge(padded, 4)
                pool.wait_ge(rope_in, 32)
                parts = 4
                with pool.Fori(0, BODIES) as i:
                    for r in range(2):
                        pool.wait_ge(ld[r], i * (16 * N_LD) + 16 * N_LD)
                        base = r * 3 * parts
                        ops = [(q[r][:, c, :], q_sw[r][:, c, :], slice(0, P)) for c in range(CHUNKS)]
                        for half in range(2):
                            rows = slice(half * HALF, (half + 1) * HALF)
                            ops.append((k[r][rows, half, 0:LAT], k_sw[r][rows, :], rows))
                        n = 0
                        for x, xs, rows in ops:
                            cos, sin = (rope[rows, j, :] for j in range(2))
                            pool.tensor_tensor(xs, xs, sin, ALU.mult).then_inc(rotated, 1)
                            pool.tensor_tensor(x, x, cos, ALU.mult).then_inc(rotated, 1)
                            n += 2
                            pool.wait_ge(rotated, i * (6 * parts) + (base + n))
                            pool.tensor_tensor(x, x, xs, ALU.add).then_inc(rotated, 1)
                            n += 1
                            pool.wait_ge(rotated, i * (6 * parts) + (base + n))

            @block.tensor
            def _(pe):
                pe.sem_inc(trans, 2)
                pe.sem_inc(out_mm, 2)
                pe.sem_inc(y_tr, 2)
                pe.wait_ge(zeroed, 1)
                pe.wait_ge(padded, 4)
                if banded:
                    pe.wait_ge(v_padded, 2)

                def values(i, r):
                    pe.wait_ge(ld[r], i * (16 * N_LD) + 16 * N_LD)
                    pe.wait_ge(y_ev, i * Y + (r * TURNED + 1))
                    for n, (a, b) in enumerate(V_GROUPS):
                        if n:
                            pe.wait_ge(v_ev, i * (2 * len(V_GROUPS)) + (r * len(V_GROUPS) + n))
                        pe.sem_inc(turning, 1)
                        for t in range(a, b):
                            rows = HEAD if banded else P
                            m = pe.transpose(ps_y[:, (t - a) * VW_:(t - a + 1) * VW_], vt[r][0:rows, t * P:(t + 1) * P],
                                             net.ident[0:rows, 0:rows])
                        m.then_inc(v_tr, 1)
                    pe.wait_ge(v_ev, i * (2 * len(V_GROUPS)) + ((r + 1) * len(V_GROUPS)))

                def score(i, u):
                    w = units[u]
                    if banded and u % UG == 0:
                        pe.wait_ge(rotated, i * 24 + 12 * (w["r"] + 1))
                    pe.wait_ge(probs, i * U + (u + 1))
                    for at, n, keys in w["keys"]:
                        m = pe.matmul(ps_s[u % 2][:, at:at + n], w["q"], keys, start=True, stop=True)
                    m.then_inc(scores, 1)

                def transpose(i, u):
                    w = units[u]
                    pe.wait_ge(pt_a, i * U + (u + 1))
                    pe.wait_ge(pt_b, i * U + (u + 1))
                    pe.wait_ge(probs, i * U + (u + 3))
                    for j, (at, n, _) in enumerate(w["blocks"]):
                        m = pe.transpose(ps_p[0:n, j * P:(j + 1) * P], prob[u % 2][:, at:at + n], net.ident)
                    m.then_inc(trans, 1)

                def output(i, u):
                    w = units[u]
                    pe.wait_ge(normed, i * U + (u + 1))
                    pe.wait_ge(pt_a, i * U + (u + 2))
                    pe.wait_ge(pt_b, i * U + (u + 2))
                    last = len(w["blocks"]) - 1
                    for j, (_, n, val) in enumerate(w["blocks"]):
                        m = pe.matmul(ps_o[:, 0:P], pt[u % 2][0:n, j * P:(j + 1) * P], val, start=(j == 0), stop=(j == last))
                    m.then_inc(out_mm, 1)

                def turn(i, y):
                    pe.wait_ge(y_ev, i * Y + (y + 1))
                    pe.wait_ge(normed, i * U + (heads * (y + 1) + 1))
                    for c in range(CHUNKS):
                        m = pe.transpose(ps_y[:, c * P:(c + 1) * P], yb[y % 2][:, c * P:(c + 1) * P], net.ident)
                    m.then_inc(y_tr, 1)

                with pe.Fori(0, BODIES) as i:
                    values(i, 0)
                    score(i, 0)
                    for u in range(U + 4):
                        if u == SWITCH:
                            values(i, 1)
                        if u + 1 < U:
                            score(i, u + 1)
                        if u < U:
                            transpose(i, u)
                        if 1 <= u <= U:
                            output(i, u - 1)
                        if u >= heads + 2 and (u - 2) % heads == 0 and (u - 2) // heads <= Y:
                            turn(i, (u - 2) // heads - 1)

            @block.scalar
            def _(act):
                act.sem_inc(probs, 2)
                act.sem_inc(pt_b, 1)
                act.sem_inc(y_ev, 1)

                def values(i, r):
                    for n, (a, b) in enumerate(V_GROUPS):
                        act.wait_ge(v_tr, i * (2 * len(V_GROUPS)) + (r * len(V_GROUPS) + n + 1))
                        act.activation(v[r][:, a:b, 0:VW_], ps_y[:, 0:(b - a) * VW_].rearrange("p (t c) -> p t c", c=VW_),
                                       ACT.Copy).then_inc(v_ev, 1)

                def exponentials(i, u):
                    w = units[u]
                    act.wait_ge(trans, i * U + (u + 1))
                    act.wait_ge(maxed, i * U + (u + 1))
                    if banded:
                        act.activation(den[:, u % 4, 1:2], sink8[w["r"]][:, w["head"]:w["head"] + 1], ACT.Exp,
                                       bias=mx[:, 2, u % 2:u % 2 + 1], scale=SCALE).then_inc(sinks, 1)
                    act.activation(prob[u % 2][:, 0:w["n"]], ps_s[u % 2][:, 0:w["n"]], ACT.Exp, bias=mx[:, 2, u % 2:u % 2 + 1],
                                   scale=SCALE, accum_out=den[:, u % 4, 0:1]).then_inc(probs, 1)

                def copy_b(i, u):
                    n = len(units[u]["blocks"])
                    act.wait_ge(out_mm, i * U + (u + 1))
                    act.wait_ge(trans, i * U + (u + 3))
                    if n > 4:
                        act.activation(pt[u % 2][:, 4 * P:n * P], ps_p[:, 4 * P:n * P], ACT.Copy).then_inc(pt_b, 1)
                    else:
                        act.sem_inc(pt_b, 1)

                def turned(i, y):
                    act.wait_ge(stored[y // YG], i * 16 + 16)
                    act.wait_ge(y_tr, i * Y + (y + 3))
                    t = y % YG
                    act.activation(yt[y // YG][:, :, t * P:(t + 1) * P], ps_y[:, 0:CHUNKS * P].rearrange("p (c t) -> p c t", c=CHUNKS),
                                   ACT.Copy).then_inc(y_ev, 1)

                with act.Fori(0, BODIES) as i:
                    values(i, 0)
                    for u in range(U + 5):
                        if 1 <= u <= U:
                            copy_b(i, u - 1)
                        if u < U:
                            exponentials(i, u)
                        if u >= heads + 3 and (u - 3) % heads == 0 and (u - 3) // heads <= Y:
                            turned(i, (u - 3) // heads - 1)
                        if u == SWITCH:
                            values(i, 1)

            @block.vector
            def _(dve):
                dve.sem_inc(pt_a, 1)
                dve.sem_inc(normed, 1)
                dve.memset(ps_p[:], 0.0).then_inc(zeroed, 1)
                if banded:
                    for r in range(2):
                        dve.memset(v[r][:, :, HEAD:P], 0.0).then_inc(v_padded, 1)
                    dve.wait_ge(rope_in, 32)
                    dve.tensor_scalar(sink_all[:], sink_all[:], 1.0 / SCALE, None, ALU.mult).then_inc(zeroed, 1)
                    dve.wait_ge(zeroed, 2)

                def maximum(i, u):
                    w = units[u]
                    s, lat, n = ps_s[u % 2], w["lat"], w["n"]
                    row = [mx[:, j, u % 2:u % 2 + 1] for j in range(3)]
                    dve.wait_ge(scores, i * U + (u + 1))
                    dve.reduce_max(row[0], s[:, lat:n], AX_X).then_inc(front, 1)
                    dve.wait_ge(front, i * F + (front_of[u] + 1))
                    if w["bias"] is not None:
                        dve.sem_inc(held, 1)
                        dve.tensor_tensor_reduce(s[:, 0:lat], s[:, 0:lat], w["bias"], 1.0, row[0], ALU.add, ALU.max, row[1])\
                           .then_inc(front, 1)
                        dve.wait_ge(front, i * F + (front_of[u] + 2))
                        top = row[1]
                    else:
                        top = row[0]
                    if banded:
                        dve.tensor_scalar(row[2], top, sink8[w["r"]][:, w["head"]:w["head"] + 1], -SCALE, ALU.max, ALU.mult)\
                           .then_inc(maxed, 1)
                    else:
                        dve.tensor_scalar(row[2], top, -SCALE, None, ALU.mult).then_inc(maxed, 1)

                def copy_a(i, u):
                    n = min(len(units[u]["blocks"]), 4)
                    dve.wait_ge(out_mm, i * U + (u + 1))
                    dve.wait_ge(trans, i * U + (u + 3))
                    dve.tensor_copy(pt[u % 2][:, 0:n * P], ps_p[:, 0:n * P]).then_inc(pt_a, 1)

                R = 2 if banded else 1

                def normalise(i, u):
                    w = units[u]
                    y = u // heads
                    d = [den[:, u % 4, j:j + 1] for j in range(3)]
                    if banded:
                        dve.tensor_tensor(d[0], d[0], d[1], ALU.add).then_inc(recip, 1)
                        dve.wait_ge(recip, i * (R * U) + (R * u + 1))
                    dve.reciprocal(d[2], d[0]).then_inc(recip, 1)
                    dve.wait_ge(y_tr, i * Y + (y + 1))
                    dve.wait_ge(out_mm, i * U + (u + 3))
                    dve.wait_ge(recip, i * (R * U) + (R * u + R))
                    dve.tensor_scalar(yb[y % 2][:, w["head"] * HEAD:(w["head"] + 1) * HEAD], ps_o[:, w["vcol"]:w["vcol"] + HEAD], d[2], None,
                                      ALU.mult).then_inc(normed, 1)

                with dve.Fori(0, BODIES) as i:
                    for u in range(U + 2):
                        if banded and u % UG == 0 and u < U:
                            r = u // UG
                            dve.tensor_scalar(sink8[r][:], sink_all[:, ds(i * (2 * GROUP) + r * GROUP, GROUP)], 1.0, None,
                                              ALU.mult).then_inc(zeroed, 1)
                            dve.wait_ge(zeroed, i * 2 + (3 + r))
                        if u < U:
                            maximum(i, u)
                        if 1 <= u <= U:
                            copy_a(i, u - 1)
                        if u >= 2:
                            normalise(i, u - 2)


def gla_stage(nc, net, name, proj, y_T):
    NT, NCH = TOK // P, TOK // CHUNK
    PAIRS = GLA_HEADS // 2
    base_q, base_k, base_v, base_r, base_z = (3 * NAW, 3 * NAW + KW, 3 * NAW + 2 * KW, 3 * NAW + 2 * KW + VW,
                                              3 * NAW + 2 * KW + 2 * VW)
    segs = [(s, min(s + 512, TOK)) for s in range(0, TOK, 512)]
    order = [list(range(LAT_TILES, NT)) + list(range(LAT_TILES)), list(range(NT - 1, LAT_TILES - 1, -1)) + list(range(LAT_TILES - 1, -1, -1))]
    halves = [(0, 1), (1, 0)]
    hp_rows = [slice(0, DK), slice(DK, 2 * DK)]
    with ExitStack() as ctx:
        sb, pb, sem = sbuf(nc, ctx), psum(nc, ctx), sems(nc, net, ctx, name)
        zt = [sb(f"{name}_zt{d}", [RANK, TOK]) for d in range(2)]
        wa = sb(f"{name}_wa", [RANK, 2, KW])
        qf, kf = sb(f"{name}_q", [P, PAIRS, TOK]), sb(f"{name}_k", [P, PAIRS, TOK])
        vf = sb(f"{name}_vf", [P, GLA_HEADS, TOK])
        kt, kd = (vf[:, n * PAIRS:(n + 1) * PAIRS, :] for n in range(2))
        v = sb(f"{name}_v", [P, NT, VW])
        sr = sb(f"{name}_sr", [P, GLA_HEADS, TOK])
        la = [sb(f"{name}_la{d}", [P, PAIRS, TOK]) for d in range(2)]
        b = sb(f"{name}_b", [P, PAIRS, TOK])
        e = sb(f"{name}_e", [P, PAIRS, TOK])
        qt = sb(f"{name}_qt", [P, PAIRS, TOK])
        kd_tok = sb(f"{name}_kd_tok", [P, NT, KW])
        o = sb(f"{name}_o", [P, NT, VW])
        state = [sb(f"{name}_state{n}", [P, GLA_HEADS, DV]) for n in range(3)]
        att = [sb(f"{name}_att{n}", [P, 2, PAIRS, P]) for n in range(2)]
        dec = sb(f"{name}_dec", [P, PAIRS, NCH])
        seg_mask = [sb(f"{name}_seg{d}", [P, TOK]) for d in range(2)]
        stat = sb(f"{name}_stat", [P, 3, NT, GLA_HEADS])
        junk = sb(f"{name}_junk", [P, DV])
        bank_z = pb(f"{name}_z", [P, 3 * 512])
        ps_a = [pb(f"{name}_ps_a{n}", [P, 512]) for n in range(2)]
        ps_d = [pb(f"{name}_ps_d{n}", [P, 512]) for n in range(2)]
        ps_o = [pb(f"{name}_ps_o", [P, 512])[:], bank_z[:, 0:512]]
        ps_t = [bank_z[:, 512:1024], bank_z[:, 1024:1536]]
        (z_in, qk_in, v_in, r_in, masks, z_mm, z_abs, z_exp, z_ln, z_min, la_done, silu, gated, v_tr, v_ev, scanned, e1, e2,
         e3, diff, qt_done, kt_done, kd_done, decs, kd_tr, kd_ev, att_mm, att_s, ds_mm, st, st_pe, o_mm, o_ev, o_sum, sq, ms,
         rstd, normed, y_tr, y_ev, stored) = (sem(n) for n in (
             "z_in", "qk_in", "v_in", "r_in", "masks", "z_mm", "z_abs", "z_exp", "z_ln", "z_min", "la_done", "silu",
             "gated", "v_tr", "v_ev", "scanned", "e1", "e2", "e3", "diff", "qt_done", "kt_done", "kd_done", "decs",
             "kd_tr", "kd_ev", "att_mm", "att_s", "ds_mm", "st", "st_pe", "o_mm", "o_ev", "o_sum", "sq", "ms", "rstd",
             "normed", "y_tr", "y_ev", "stored"))
        KG = NT // 2
        chunked = lambda x: x.rearrange("p a (n c) -> p a n c", c=CHUNK)

        def last_of(d):
            edge = CHUNK - 1 if d == 0 else 0
            return chunked(b[:])[:, :, :, edge:edge + 1]

        with nc.Block() as block:
            @block.sync
            def _(sp):
                rows = lambda base, n: proj[base:base + n, :]
                for d in range(2):
                    sp.dma_start(zt[d][:], rows(base_z + d * RANK, RANK)).then_inc(z_in, 16)
                sp.dma_start(wa[:], net.gla_wa2[0].rearrange("d k n -> k d n")).then_inc(z_in, 16)
                sp.dma_start(vf[:], rows(base_v, VW).rearrange("(h p) t -> p h t", p=P)).then_inc(v_in, 16)
                sp.dma_start(qf[:], rows(base_q, KW).rearrange("(h p) t -> p h t", p=P)).then_inc(qk_in, 16)
                sp.dma_start(kf[:], rows(base_k, KW).rearrange("(h p) t -> p h t", p=P)).then_inc(qk_in, 16)
                sp.dma_start(sr[:], rows(base_r, VW).rearrange("(h p) t -> p h t", p=P)).then_inc(r_in, 16)
                out = y_T[NAW:D, :].rearrange("(h p) t -> p h t", p=P)
                cut = LAT_TILES // 2
                sp.wait_ge(y_ev, NT - cut)
                sp.dma_start(out[:, :, cut * P:TOK], sr[:, :, cut * P:TOK]).then_inc(stored, 16)
                sp.wait_ge(y_ev, NT)
                sp.dma_start(out[:, :, 0:cut * P], sr[:, :, 0:cut * P]).then_inc(stored, 16)
                sp.wait_ge(stored, 32)

            @block.gpsimd
            def _(pool):
                clear_last_stage(pool, net)
                for d in range(2):
                    pool.memset(seg_mask[d][:], 1.0).then_inc(masks, 1)
                for n in range(3):
                    pool.memset(state[n][:], 0.0).then_inc(masks, 1)
                pool.wait_ge(masks, 5)
                for d, edge in enumerate((0, CHUNK - 1)):
                    m = seg_mask[d][:].rearrange("p (n c) -> p n c", c=CHUNK)[:, :, edge:edge + 1]
                    pool.memset(m, 0.0).then_inc(masks, 1)
                for n, t in enumerate(order[1]):
                    pool.wait_ge(ms, n + 1)
                    pool.tensor_tensor(stat[:, 2, t, :], stat[:, 1, t, :], net.half[:, 0:GLA_HEADS], ALU.pow).then_inc(rstd, 1)

            @block.tensor
            def _(pe):
                pe.wait_ge(z_in, 48)
                for n in range(2 * PAIRS):
                    d, c = divmod(n, PAIRS)
                    if n:
                        pe.wait_ge(z_min, n)
                    for a, z in segs:
                        m = pe.matmul(bank_z[:, a:z], wa[:, d, c * P:(c + 1) * P], zt[d][:, a:z], start=True, stop=True)
                    m.then_inc(z_mm, 1)
                pe.wait_ge(z_min, 2 * PAIRS)
                pe.wait_ge(v_in, 16)
                for t in range(NT):
                    if t >= 2:
                        pe.wait_ge(v_ev, t - 1)
                    for h in range(GLA_HEADS):
                        m = pe.transpose(ps_t[t % 2][:, h * P:(h + 1) * P], vf[:, h, t * P:(t + 1) * P], net.ident)
                    m.then_inc(v_tr, 1)
                pe.wait_ge(v_ev, NT)
                pe.wait_ge(masks, 7)

                def turn_kd(d):
                    pe.wait_ge(kd_done, d + 1)
                    if d:
                        pe.wait_ge(o_ev, NT)
                    for g in range(KG):
                        G = d * KG + g
                        if G >= 2:
                            pe.wait_ge(kd_ev, G - 1)
                        for t in (2 * g, 2 * g + 1):
                            for c in range(PAIRS):
                                m = pe.transpose(ps_t[G % 2][:, ((t % 2) * PAIRS + c) * P:((t % 2) * PAIRS + c + 1) * P],
                                                 kd[:, c, t * P:(t + 1) * P], net.ident)
                        m.then_inc(kd_tr, 1)
                    pe.wait_ge(kd_ev, (d + 1) * KG)

                def scores(N, d, t):
                    if N:
                        pe.wait_ge(att_s, 2 * N)
                    for hp in range(2):
                        for c in range(PAIRS):
                            m = pe.matmul(ps_a[hp][:, c * P:(c + 1) * P], kt[hp_rows[hp], c, t * P:(t + 1) * P],
                                          qt[hp_rows[hp], c, t * P:(t + 1) * P], start=True, stop=True)
                    m.then_inc(att_mm, 1)

                def increments(N, d, t):
                    for x, half in enumerate(halves[d]):
                        J = 2 * N + x
                        if J >= 2:
                            pe.wait_ge(st, 4 * (J - 1))
                        rows = hp_rows[half]
                        for h in range(GLA_HEADS):
                            c, hp = divmod(h, 2)
                            m = pe.matmul(ps_d[half][hp_rows[hp], c * DV:(c + 1) * DV], kd_tok[rows, t, h * DK:(h + 1) * DK],
                                          v[rows, t, h * DV:(h + 1) * DV], start=True, stop=True)
                        m.then_inc(ds_mm, 1)

                def outputs(N, d, t):
                    bank = ps_o[N % 2]
                    if 2 <= N < NT:
                        pe.wait_ge(o_ev, N - 1)
                    elif N >= NT + 2:
                        pe.wait_ge(o_sum, N - NT - 1)
                    pe.wait_ge(att_s, 2 * N + 2)
                    for h in range(GLA_HEADS):
                        c, hp = divmod(h, 2)
                        pe.matmul(bank[:, h * DV:(h + 1) * DV], att[N % 2][:, hp, c, :], v[:, t, h * DV:(h + 1) * DV],
                                  start=(h == 0), stop=False, skip_group_check=True)
                    for x, half in enumerate(halves[d]):
                        J = 2 * N + x
                        if J:
                            pe.wait_ge(st, 4 * J)
                        for h in range(GLA_HEADS):
                            m = pe.matmul(bank[hp_rows[half], h * DV:(h + 1) * DV],
                                          qt[:, h // 2, t * P + half * CHUNK:t * P + (half + 1) * CHUNK], state[J % 3][:, h, :],
                                          start=False, stop=(x == 1), skip_group_check=True)
                        m.then_inc(st_pe, 1)
                    pe.wait_ge(st_pe, 2 * N + 2)
                    pe.sem_inc(o_mm, 1)

                def turn_out(n):
                    t = order[1][n]
                    pe.wait_ge(normed, n + 1)
                    if n >= 2:
                        pe.wait_ge(y_ev, n - 1)
                    for h in range(GLA_HEADS):
                        m = pe.transpose(ps_t[n % 2][:, h * P:(h + 1) * P], o[:, t, h * DV:(h + 1) * DV], net.ident)
                    m.then_inc(y_tr, 1)

                for d in range(2):
                    turn_kd(d)
                    pe.wait_ge(kt_done, d + 1)
                    scores(d * NT, d, order[d][0])
                    for n, t in enumerate(order[d]):
                        N = d * NT + n
                        increments(N, d, t)
                        if n + 1 < NT:
                            scores(N + 1, d, order[d][n + 1])
                        outputs(N, d, t)
                        if d and n >= 2:
                            turn_out(n - 2)
                turn_out(NT - 2)
                turn_out(NT - 1)

            @block.scalar
            def _(act):
                act.wait_ge(r_in, 16)
                act.activation(sr[:], sr[:], ACT.Silu).then_inc(silu, 1)
                for n in range(2 * PAIRS):
                    d, c = divmod(n, PAIRS)
                    ba = param(net, "gla_ba", n, 1)
                    act.wait_ge(z_mm, n + 1)
                    if n >= 2:
                        act.wait_ge(la_done, n - 1)
                    x = e[:, n % 2, :]
                    act.activation(x, bank_z[:, 0:TOK], ACT.Abs, bias=ba).then_inc(z_abs, 1)
                    act.wait_ge(z_abs, n + 1)
                    act.activation(x, x, ACT.Exp, scale=-1.0).then_inc(z_exp, 1)
                    act.wait_ge(z_exp, n + 1)
                    act.activation(x, x, ACT.Ln, bias=1.0).then_inc(z_ln, 1)
                for t in range(NT):
                    act.wait_ge(v_tr, t + 1)
                    act.activation(v[:, t, :], ps_t[t % 2], ACT.Copy).then_inc(v_ev, 1)
                act.wait_ge(la_done, 2 * PAIRS)
                for d in range(2):
                    act.wait_ge(scanned, 2 * (d + 1))
                    if d:
                        act.wait_ge(kt_done, d)
                        act.wait_ge(st, 4 * NCH)
                    act.activation(e[:], b[:], ACT.Exp, scale=1.0 / TAU).then_inc(e1, 1)
                    act.activation(dec[:].unsqueeze(3), last_of(d), ACT.Exp, scale=1.0 / TAU).then_inc(decs, 1)
                    act.wait_ge(diff, d + 1)
                    act.activation(kd, kd, ACT.Exp, scale=1.0 / TAU).then_inc(e3, 1)
                    act.wait_ge(qt_done, d + 1)
                    act.activation(e[:], b[:], ACT.Exp, scale=-1.0 / TAU).then_inc(e2, 1)
                    for g in range(KG):
                        G = d * KG + g
                        act.wait_ge(kd_tr, G + 1)
                        if d and not g:
                            act.wait_ge(ds_mm, NCH)
                        act.activation(kd_tok[:, 2 * g:2 * g + 2, :], ps_t[G % 2].rearrange("p (t n) -> p t n", t=2),
                                       ACT.Copy).then_inc(kd_ev, 1)
                    for n, t in enumerate(order[d]):
                        if d == 0:
                            act.wait_ge(o_mm, n + 1)
                            act.activation(o[:, t, :], ps_o[n % 2], ACT.Copy).then_inc(o_ev, 1)
                        else:
                            act.wait_ge(o_sum, n + 1)
                            for h in range(GLA_HEADS):
                                if n or h:
                                    act.wait_ge(sq, GLA_HEADS * n + h)
                                act.activation(junk[:], o[:, t, h * DV:(h + 1) * DV], ACT.Square,
                                               accum_out=stat[:, 0, t, h:h + 1]).then_inc(sq, 1)

            @block.vector
            def _(dve):
                for n in range(2 * PAIRS):
                    d, c = divmod(n, PAIRS)
                    dve.wait_ge(z_abs, n + 1)
                    dve.tensor_scalar(la[d][:, c, :], bank_z[:, 0:TOK], param(net, "gla_ba", n, 1), 0.0, ALU.add, ALU.min)\
                       .then_inc(z_min, 1)
                    dve.wait_ge(z_ln, n + 1)
                    dve.wait_ge(z_min, n + 1)
                    dve.tensor_tensor(la[d][:, c, :], la[d][:, c, :], e[:, n % 2, :], ALU.subtract).then_inc(la_done, 1)
                dve.wait_ge(silu, 1)
                for h in range(GLA_HEADS):
                    dve.tensor_scalar(sr[:, h, :], sr[:, h, :], param(net, "gla_g", h, 1), None, ALU.mult).then_inc(gated, 1)
                dve.wait_ge(qk_in, 32)
                dve.wait_ge(masks, 7)
                dve.wait_ge(la_done, 2 * PAIRS)
                tri = [net.const[:, CCOL[n]:CCOL[n] + P].unsqueeze(1).to_broadcast([P, PAIRS, P]) for n in ("tri_f", "tri_b")]
                for d in range(2):
                    if d:
                        dve.wait_ge(e2, d)
                    for c in range(PAIRS):
                        rev = slice(None, None, -1) if d else slice(None)
                        dve.tensor_tensor_scan(b[:, c, rev], seg_mask[d][:, rev], la[d][:, c, rev], 0.0, ALU.mult, ALU.add)\
                           .then_inc(scanned, 1)
                    dve.wait_ge(scanned, 2 * (d + 1))
                    if d:
                        dve.wait_ge(kd_tr, KG)
                    else:
                        dve.wait_ge(v_tr, NT)
                    dve.tensor_tensor(chunked(kd), last_of(d).to_broadcast([P, PAIRS, NCH, CHUNK]), chunked(b[:]),
                                      ALU.subtract).then_inc(diff, 1)
                    if d:
                        dve.wait_ge(o_mm, NT)
                    dve.wait_ge(e1, d + 1)
                    dve.scalar_tensor_tensor(qt[:], qf[:], DK ** -0.5, e[:], ALU.mult, ALU.mult).then_inc(qt_done, 1)
                    dve.wait_ge(e3, d + 1)
                    dve.tensor_tensor(kd, kd, kf[:], ALU.mult).then_inc(kd_done, 1)
                    dve.wait_ge(e2, d + 1)
                    dve.tensor_tensor(kt, kf[:], e[:], ALU.mult).then_inc(kt_done, 1)
                    dve.wait_ge(decs, d + 1)

                    def mask(N):
                        dve.wait_ge(att_mm, N + 1)
                        if N >= 2:
                            dve.wait_ge(o_mm, N - 1)
                        for hp in range(2):
                            dve.tensor_tensor(att[N % 2][:, hp], ps_a[hp][:, 0:PAIRS * P].rearrange("p (c q) -> p c q", c=PAIRS),
                                              tri[d], ALU.mult).then_inc(att_s, 1)

                    def finish(n):
                        t = order[1][n]
                        dve.wait_ge(sq, GLA_HEADS * (n + 1))
                        dve.tensor_scalar(stat[:, 1, t, :], stat[:, 0, t, :], 1.0 / DV, EPS, ALU.mult, ALU.add).then_inc(ms, 1)
                        dve.wait_ge(rstd, n + 1)
                        ot = o[:, t, :].rearrange("p (h v) -> p h v", h=GLA_HEADS)
                        dve.tensor_tensor(ot, ot, stat[:, 2, t, :].unsqueeze(2).to_broadcast([P, GLA_HEADS, DV]), ALU.mult)\
                           .then_inc(normed, 1)

                    def gate(n):
                        t = order[1][n]
                        dve.wait_ge(y_tr, n + 1)
                        if not n:
                            dve.wait_ge(gated, GLA_HEADS)
                        place = sr[:, :, t * P:(t + 1) * P]
                        dve.tensor_tensor(place, ps_t[n % 2].rearrange("p (h t) -> p h t", h=GLA_HEADS), place, ALU.mult)\
                           .then_inc(y_ev, 1)

                    mask(d * NT)
                    for n, t in enumerate(order[d]):
                        N = d * NT + n
                        for x, half in enumerate(halves[d]):
                            J = 2 * N + x
                            dve.wait_ge(ds_mm, J + 1)
                            if J >= 2:
                                dve.wait_ge(st_pe, J - 1)
                            if J:
                                dve.wait_ge(st, 4 * J)
                            ci = 2 * t + half
                            for h in range(GLA_HEADS):
                                c, hp = divmod(h, 2)
                                new = state[(J + 1) % 3][hp_rows[hp], h, :]
                                if J + 1 == NCH:
                                    dve.memset(new, 0.0).then_inc(st, 1)
                                else:
                                    dve.scalar_tensor_tensor(new, state[J % 3][hp_rows[hp], h, :], dec[hp_rows[hp], c, ci:ci + 1],
                                                             ps_d[half][hp_rows[hp], c * DV:(c + 1) * DV], ALU.mult, ALU.add)\
                                       .then_inc(st, 1)
                        if n + 1 < NT:
                            mask(N + 1)
                        if d:
                            dve.wait_ge(o_mm, N + 1)
                            dve.tensor_tensor(o[:, t, :], ps_o[N % 2], o[:, t, :], ALU.add).then_inc(o_sum, 1)
                            dve.wait_ge(o_sum, n + 1)
                            if n >= 1:
                                finish(n - 1)
                            if n >= 3:
                                gate(n - 3)
                    if d:
                        gate(NT - 3)
                        finish(NT - 1)
                        gate(NT - 2)
                        gate(NT - 1)


SCRATCH = {"proj0": (IN_AB, TOK), "y0": (D, TOK), "x1": (TOK, D), "hid0": (DFF, TOK), "x2": (TOK, D),
           "proj1": (IN_C, TOK), "y1": (D, TOK), "x3": (LAT, D), "hid1": (DFF, TOK),
           "bias": (NA_HEADS, P, BIAS_COLS), "rpb_rows": (P, P),
           "mod": (DEPTH, 2, 6 * D)}


def trunk(nc, ins, out, scratch):
    net = Net(ins, scratch)
    net.this_stage = []
    with ExitStack() as ctx:
        sb = sbuf(nc, ctx)
        net.const = sb("const", [P, N_CONST])
        net.pcol = sb("pcol", [P, N_PCOL])
        net.shift, net.scale, net.gate = (sb(n, [P, DEPTH, 2, KD, 2]) for n in ("shift", "scale", "gate"))
        net.conv = sb("conv", [P, DEPTH, 2 * FT, 4])
        net.half = sb("half", [P, 4])
        net.tile_stored = [ctx.enter_context(nc.semaphore(f"tile_stored{n}")) for n in range(2)]
        net.tiles_stored = 0
        net.pad_in, net.pad_out, net.slid_in, net.b_stored = (
            ctx.enter_context(nc.semaphore(n)) for n in ("pad_in", "pad_out", "slid_in", "b_stored"))
        net.ident = net.const[:, CCOL["ident"]:CCOL["ident"] + P]
        tiles = lambda ap, n: [ap[t * P:(t + 1) * P, :] for t in range(n)]
        x0 = tiles(net.x[0], LAT_TILES) + tiles(net.ctx[0], CTX_TILES)
        x1, x2 = tiles(net.x1_d, LAT_TILES + CTX_TILES), tiles(net.x2_d, LAT_TILES + CTX_TILES)
        x3, x4 = tiles(net.x3_d, LAT_TILES), tiles(out[0], LAT_TILES)
        setup_stage(nc, net)
        project_stage(nc, net, "in0", 0, 0, x0, net.w_in_ab[0], net.proj0_d, "plain", (IN_AB - 2 * RANK) // (2 * P),
                      tail=(IN_AB - P, IN_AB - 2 * RANK))
        attention_stage(nc, net, "na", net.proj0_d, net.y0_d, False)
        gla_stage(nc, net, "gla", net.proj0_d, net.y0_d)
        close_stage(nc, net, "out0", 0, 0, net.y0_d, net.w_out[0], D, x0, x1)
        project_stage(nc, net, "up0", 0, 1, x1, net.w_up[0], net.hid0_d, "ffn", FT)
        close_stage(nc, net, "down0", 0, 1, net.hid0_d, net.w_down[0], DFF, x1, x2)
        project_stage(nc, net, "in1", 1, 0, x2, net.w_in_c[0], net.proj1_d, "plain", IN_C // (2 * P))
        attention_stage(nc, net, "swa", net.proj1_d, net.y1_d, True)
        close_stage(nc, net, "out1", 1, 0, net.y1_d, net.w_out[1], D, x2[:LAT_TILES], x3)
        project_stage(nc, net, "up1", 1, 1, x3, net.w_up[1], net.hid1_d, "ffn", FT)
        close_stage(nc, net, "down1", 1, 1, net.hid1_d, net.w_down[1], DFF, x3, x4)


_INS = ["x", "c", "ctx", "c_ctx", "w_mod", "b_mod", "g_mix_pre", "g_mix_post", "g_ffn_pre", "g_ffn_post", "w_out", "w_up",
        "conv_w", "conv_b", "w_down", "w_in_ab", "na_rpb", "gla_wa2", "gla_ba", "gla_g", "w_in_c", "swa_sink"]


def constants():
    import numpy as np

    i, j = np.arange(P)[:, None], np.arange(P)[None, :]
    cq, ck = np.arange(P)[:, None] % GRID_W, np.arange(GRID_W)[None, :]
    start = np.clip(cq - NA_WIN // 2, 0, GRID_W - NA_WIN)
    ok = (ck >= start) & (ck < start + NA_WIN)
    same = (i // CHUNK) == (j // CHUNK)
    key = np.arange(3 * P)[None, :] - P
    parts = {
        "ident": i == j,
        "flip": (i < GRID_W) & (j % GRID_W == GRID_W - 1 - i),
        "tri_f": same & (i <= j), "tri_b": same & (i >= j),
        "na_ok": ok, "na_neg": np.where(ok, 0.0, 8 * NEG),
        "swa_mask": np.where(np.abs(i - key) <= 128, 0.0, 8 * NEG),
    }
    const = np.concatenate([parts[name].astype(np.float32) for name, _ in CONST_COLS], axis=1)
    t = np.arange(LAT)
    inv = (1.0 / (np.float32(10000.0) ** (np.arange(0, HEAD // 2, 2, dtype=np.float32) / np.float32(HEAD // 2)))).astype(np.float32)
    ang = np.concatenate([(t // GRID_W).astype(np.float32)[:, None] * inv, (t % GRID_W).astype(np.float32)[:, None] * inv], -1)
    cos, sin = np.cos(ang).T, np.sin(ang).T
    pair = (np.arange(P) % HEAD) // 2
    sign = np.where(np.arange(P) % 2 == 0, -1.0, 1.0)[:, None]
    rope = np.stack([cos[pair], sin[pair] * sign]).astype(np.float32)
    return const, rope


def kernel(**inputs):
    import numpy as np
    import concourse.bacc as bacc
    from concourse.bass_utils import run_bass_kernel_spmd

    nc = bacc.Bacc("TRN2", target_bir_lowering=False, num_devices=1)
    const, rope = constants()
    arrays = {f"in_{n}": np.ascontiguousarray(inputs[n]) for n in _INS}
    arrays["in_const_d"], arrays["in_rope_d"] = const, rope
    ins = {n[3:]: nc.dram_tensor(n, a.shape, mybir.dt.from_np(a.dtype), kind="ExternalInput").ap() for n, a in arrays.items()}
    scratch = {n: nc.dram_tensor(f"scratch_{n}", shape, F32, kind="Internal").ap() for n, shape in SCRATCH.items()}
    out = nc.dram_tensor("out_0", (1, LAT, D), F32, kind="ExternalOutput").ap()
    trunk(nc, ins, out, scratch)
    r = run_bass_kernel_spmd(nc, [arrays], core_ids=[0])
    return r.results[0]["out_0"]
```

```python
from contextlib import ExitStack

import concourse.bass as bass
from concourse import mybir
from concourse.alu_op_type import AluOpType as ALU

ACT = mybir.ActivationFunctionType
AX_X = mybir.AxisListType.X
F32 = mybir.dt.float32
F32R = mybir.dt.float32r
ds = bass.ds

P = 128
D = 1024
KD = D // P
LAT, CTXN = 1024, 256
TOK = LAT + CTXN
LAT_TILES, CTX_TILES = LAT // P, CTXN // P
GRID_W = 64
HEAD = 64
DEPTH = 2
NA_HEADS, NA_ROWS, NA_WIN = 8, 8, 16
NAW = NA_HEADS * HEAD
GLA_HEADS, DK, DV, CHUNK, RANK = 4, 64, 128, 64, 16
KW, VW = GLA_HEADS * DK, GLA_HEADS * DV
IN_AB = 3 * NAW + 2 * KW + 2 * VW + 2 * RANK
SWA_HEADS, KV, GROUP = 16, 4, 4
IN_C = (SWA_HEADS + 2 * KV) * HEAD
DFF = 2816
FT = DFF // P
TAU = 16.0
EPS = 1e-6
NEG = -1e30
SCALE = HEAD ** -0.5

PARAM_ROWS = [("c", KD), ("c_ctx", KD), ("b_mod", DEPTH * 6 * KD), ("g_mix_pre", DEPTH * KD),
              ("g_ffn_pre", DEPTH * KD), ("conv_w", DEPTH * 3 * 2 * FT),
              ("conv_b", DEPTH * 2 * FT), ("gla_ba", 2 * KW // P), ("gla_g", VW // P)]
PCOL, _at = {}, 0
for _name, _count in PARAM_ROWS:
    PCOL[_name] = _at
    _at += _count
N_PCOL = _at
P_TILES = -(-N_PCOL // P)

CONST_COLS = [("ident", P), ("flip", P), ("tri_f", P), ("tri_b", P), ("na_neg", GRID_W),
              ("swa_mask", 3 * P), ("four", 2)]
CCOL, _at = {}, 0
for _name, _count in CONST_COLS:
    CCOL[_name] = _at
    _at += _count
N_CONST = _at

EDGE_SLOTS, INNER_SLOTS = 15, 9
BIAS_COLS = (EDGE_SLOTS + INNER_SLOTS) * GRID_W


class Net:

    def __init__(self, ins, scratch):
        self.x, self.c, self.ctx, self.c_ctx, self.w_mod, self.b_mod = (
            ins[n] for n in ("x", "c", "ctx", "c_ctx", "w_mod", "b_mod"))
        self.g_mix_pre, self.g_mix_post, self.g_ffn_pre, self.g_ffn_post, self.w_out, self.w_up = (
            ins[n] for n in ("g_mix_pre", "g_mix_post", "g_ffn_pre", "g_ffn_post", "w_out", "w_up"))
        self.conv_w, self.conv_b, self.w_down, self.w_in_ab, self.na_rpb, self.gla_wa2 = (
            ins[n] for n in ("conv_w", "conv_b", "w_down", "w_in_ab", "na_rpb", "gla_wa2"))
        self.gla_ba, self.gla_g, self.w_in_c, self.swa_sink, self.const_d, self.rope_d = (
            ins[n] for n in ("gla_ba", "gla_g", "w_in_c", "swa_sink", "const_d", "rope_d"))
        self.proj0_d, self.y0_d, self.x1_d, self.hid0_d, self.x2_d, self.proj1_d = (
            scratch[n] for n in ("proj0", "y0", "x1", "hid0", "x2", "proj1"))
        self.y1_d, self.x3_d, self.hid1_d, self.bias_d, self.rpb_rows_d, self.mod_d = (
            scratch[n] for n in ("y1", "x3", "hid1", "bias", "rpb_rows", "mod"))


def sbuf(nc, ctx):
    return lambda name, shape, dt=F32: ctx.enter_context(nc.sbuf_tensor(name, shape, dt))


def psum(nc, ctx):
    return lambda name, shape: ctx.enter_context(nc.psum_tensor(name, shape, F32))


def sems(nc, net, ctx, stage):
    net.last_stage, net.this_stage = net.this_stage, []

    def make(name):
        s = ctx.enter_context(nc.semaphore(f"{stage}_{name}"))
        net.this_stage.append(s.num)
        return s
    return make


def clear_last_stage(pool, net):
    numbers = sorted(net.last_stage)
    while numbers:
        n = 1
        while n < len(numbers) and numbers[n] == numbers[0] + n:
            n += 1
        pool.sem_clear(range(numbers[0], numbers[0] + n))
        numbers = numbers[n:]


def param(net, name, first, count):
    return net.pcol[:, PCOL[name] + first:PCOL[name] + first + count]


def param_runs(net):
    src = {
        "c": net.c.rearrange("b (r p) -> (b r) p", p=P), "c_ctx": net.c_ctx.rearrange("(r p) -> r p", p=P),
        "b_mod": net.b_mod.rearrange("l (r p) -> (l r) p", p=P),
        "g_mix_pre": net.g_mix_pre.rearrange("l (r p) -> (l r) p", p=P),
        "g_ffn_pre": net.g_ffn_pre.rearrange("l (r p) -> (l r) p", p=P),
        "conv_w": net.conv_w.rearrange("l t (r p) -> (l t r) p", p=P),
        "conv_b": net.conv_b.rearrange("l (r p) -> (l r) p", p=P),
        "gla_ba": net.gla_ba.rearrange("n z (r p) -> (n z r) p", p=P),
        "gla_g": net.gla_g.rearrange("n (r p) -> (n r) p", p=P),
    }
    for name, count in PARAM_ROWS:
        done = 0
        while done < count:
            at = PCOL[name] + done
            n = min(count - done, P - at % P)
            yield at // P, at % P, n, src[name][done:done + n]
            done += n


def setup_stage(nc, net):
    SLOTS = 4
    CHUNKS = 6 * D // 512
    MROWS = 2 * 6 * KD
    with ExitStack() as ctx:
        sb, pb, sem = sbuf(nc, ctx), psum(nc, ctx), sems(nc, net, ctx, "setup")
        rows = sb("param_rows", [P, P_TILES, P])
        cond = sb("cond", [P, KD, 2])
        wm = [sb(f"w_mod{r}", [P, KD, 512]) for r in range(SLOTS)]
        mod_row = sb("mod_row", [2, DEPTH, 6 * D])
        mod_rows = sb("mod_rows", [MROWS, DEPTH, P])
        mod = sb("mod", [P, DEPTH, 6 * KD, 2])
        ps_cols = pb("ps_cols", [P, P_TILES, P])
        ps_mod = [pb(f"ps_mod{r}", [P, 512]) for r in range(2)]
        ps_sum = [pb(f"ps_sum{r}", [P, 512]) for r in range(2)]
        partial = [sb(f"partial{r}", [P, 512]) for r in range(2)]
        BR = NA_HEADS * EDGE_SLOTS
        pad = sb("rpb_pad", [BR, P])
        slid = sb("rpb_slid", [GRID_W, BR, GRID_W])
        table = sb("rpb_table", [P, BR, GRID_W])
        never = sb("never", [P, NA_HEADS, GRID_W])
        ps_b = [pb(f"ps_b{r}", [P, 512]) for r in range(2)]
        pad_set, b_mm, b_done = sem("pad_set"), sem("b_mm"), sem("b_done")
        pad_in, pad_out, slid_in, b_stored = net.pad_in, net.pad_out, net.slid_in, net.b_stored
        B_STEPS = BR * GRID_W // 512
        const_in, rows_in = sem("const_in"), sem("rows_in")
        w_in = [sem(f"w_in{r}") for r in range(SLOTS)]
        row_out = [sem(f"row_out{n}") for n in range(DEPTH)]
        rows_back, mod_t, part_out, summed, zeroed = (sem(n) for n in ("rows_back", "mod_t", "part_out", "summed", "zeroed"))
        cols_t, cols_done, cond_done = sem("cols_t"), sem("cols_done"), sem("cond_done")
        chunk_done, chunk_out, derived, half_set = (sem(n) for n in ("chunk_done", "chunk_out", "derived", "half_set"))
        runs = list(param_runs(net))
        with nc.Block() as block:
            @block.sync
            def _(sp):
                sp.dma_start(net.const[:], net.const_d).then_inc(const_in, 16)
                for tile, part, n, src in runs:
                    sp.dma_start(rows[part:part + n, tile, :], src).then_inc(rows_in, 16)
                for layer in range(DEPTH):
                    w = net.w_mod[layer].rearrange("(k p) n -> p k n", p=P)
                    with sp.Fori(0, CHUNKS // SLOTS) as i:
                        for r in range(SLOTS):
                            sp.wait_ge(chunk_done, i * SLOTS + (layer * CHUNKS + r + 1))
                            sp.dma_start(wm[r][:], w[:, :, ds(i * (SLOTS * 512) + r * 512, 512)]).then_inc(w_in[r], 16)
                for layer in range(DEPTH):
                    sp.wait_ge(chunk_out, 2 + (layer + 1) * CHUNKS)
                    sp.dma_start(net.mod_d[layer], mod_row[:, layer, :]).then_inc(row_out[layer], 16)
                for layer in range(DEPTH):
                    sp.wait_ge(row_out[layer], 16)
                    sp.dma_start(mod_rows[:, layer, :], net.mod_d[layer].rearrange("s (j p) -> (s j) p", p=P)).then_inc(rows_back, 16)

            @block.tensor
            def _(pe):
                pe.sem_inc(chunk_done, SLOTS)
                pe.sem_inc(summed, 2)
                pe.wait_ge(zeroed, 2)
                pe.wait_ge(const_in, 16)
                pe.wait_ge(rows_in, 16 * len(runs))
                for i in range(P_TILES):
                    n = min(P, N_PCOL - i * P)
                    t = pe.transpose(ps_cols[:, i, 0:n], rows[0:n, i, :], net.ident[0:n, 0:n])
                t.then_inc(cols_t, 1)
                pe.wait_ge(cond_done, 1)
                for layer in range(DEPTH):
                    with pe.Fori(0, CHUNKS // SLOTS) as i:
                        for r in range(SLOTS):
                            pe.wait_ge(w_in[r], i * 16 + 16 * (layer * CHUNKS // SLOTS + 1))
                            pe.wait_ge(part_out, i * SLOTS + (layer * CHUNKS + r + 1))
                            for k in range(KD):
                                at = 32 * (k % 4)
                                m = pe.matmul(ps_mod[r % 2][at:at + 2, :], cond[:, k, :], wm[r][:, k, :], start=(k < 4), stop=(k >= 4))
                            m.then_inc(chunk_done, 1)
                            pe.wait_ge(part_out, i * SLOTS + (layer * CHUNKS + r + 3))
                            pe.wait_ge(chunk_out, i * SLOTS + (layer * CHUNKS + r + 1))
                            pe.matmul(ps_sum[r % 2][0:2, :], net.const[:, CCOL["four"]:CCOL["four"] + 2], partial[r % 2][:],
                                      start=True, stop=True).then_inc(summed, 1)
                    if layer == 0:
                        pe.wait_ge(slid_in, 16)
                        flat = slid[:].rearrange("p r c -> p (r c)")
                        for n in range(B_STEPS):
                            if n >= 2:
                                pe.wait_ge(b_done, n - 1)
                            pe.matmul(ps_b[n % 2][:], net.const[0:GRID_W, CCOL["flip"]:CCOL["flip"] + P],
                                      flat[:, n * 512:(n + 1) * 512], start=True, stop=True).then_inc(b_mm, 1)

                pe.wait_ge(rows_back, 16 * DEPTH)
                for layer in range(DEPTH):
                    m = pe.transpose(ps_mod[0][:, layer * P:layer * P + MROWS], mod_rows[:, layer, :], net.ident[0:MROWS, 0:MROWS])
                m.then_inc(mod_t, 1)

            @block.gpsimd
            def _(pool):
                clear_last_stage(pool, net)
                pool.memset(net.half[:], -0.5).then_inc(half_set, 1)
                pool.memset(never[:], 8 * NEG).then_inc(half_set, 1)
                pool.memset(pad[:], 0.0).then_inc(pad_set, 1)
                pool.wait_ge(pad_set, 1)
                width = 2 * NA_WIN - 1
                at = GRID_W - NA_WIN
                pool.dma_start(pad[:, at:at + width], net.na_rpb[0].rearrange("h r c -> (h r) c")).then_inc(pad_in, 16)
                pool.wait_ge(pad_in, 16)
                pool.dma_start(net.rpb_rows_d[0:BR, :], pad[:]).then_inc(pad_out, 16)
                pool.wait_ge(pad_out, 16)
                rows_d = net.rpb_rows_d
                slide = bass.AP(tensor=rows_d.tensor, offset=rows_d.offset, ap=[[1, GRID_W], [P, BR], [1, GRID_W]])
                pool.dma_start(slid[:], slide).then_inc(slid_in, 16)
                pool.wait_ge(b_done, B_STEPS)
                pool.wait_ge(half_set, 2)
                W, H = GRID_W, P // 2
                t4 = table[:].rearrange("p (h r) c -> p h (r c)", h=NA_HEADS)
                dst = net.bias_d.rearrange("h p n -> p h n")
                inner = EDGE_SLOTS * W
                pieces = [(dst[0:H, :, 0:15 * W], t4[0:H]), (dst[H:P, :, W:15 * W], t4[H:P, :, 0:14 * W]),
                          (dst[H:P, :, 0:W], never[H:P]),
                          (dst[0:H, :, inner:inner + 8 * W], t4[0:H, :, 3 * W:11 * W]),
                          (dst[0:H, :, inner + 8 * W:inner + 9 * W], never[0:H]),
                          (dst[H:P, :, inner + W:inner + 9 * W], t4[H:P, :, 3 * W:11 * W]),
                          (dst[H:P, :, inner:inner + W], never[H:P])]
                for to, what in pieces:
                    pool.dma_start(to, what).then_inc(b_stored, 16)
                pool.wait_ge(b_stored, 16 * len(pieces))

            @block.scalar
            def _(act):
                act.wait_ge(cols_done, 1)
                act.activation(cond[:], param(net, "c", 0, 2 * KD).rearrange("p (s k) -> p k s", s=2), ACT.Silu).then_inc(cond_done, 1)

            @block.vector
            def _(dve):
                dve.sem_inc(chunk_out, 2)
                dve.sem_inc(part_out, 2)
                for r in range(2):
                    dve.memset(ps_mod[r][:], 0.0).then_inc(zeroed, 1)
                dve.wait_ge(cols_t, 1)
                dve.tensor_copy(net.pcol[:], ps_cols[:].rearrange("p i n -> p (i n)")[:, 0:N_PCOL]).then_inc(cols_done, 1)
                for layer in range(DEPTH):
                    with dve.Fori(0, CHUNKS // SLOTS) as i:
                        for r in range(SLOTS):
                            dve.wait_ge(chunk_done, i * SLOTS + (layer * CHUNKS + r + 1 + SLOTS))
                            dve.wait_ge(summed, i * SLOTS + (layer * CHUNKS + r + 1))
                            dve.tensor_scalar(partial[r % 2][:], ps_mod[r % 2][:], 1.0, None, ALU.mult).then_inc(part_out, 1)
                            dve.wait_ge(summed, i * SLOTS + (layer * CHUNKS + r + 3))
                            dst = mod_row[:, layer, ds(i * (SLOTS * 512) + r * 512, 512)]
                            dve.tensor_scalar(dst, ps_sum[r % 2][0:2, :], 1.0, None, ALU.mult).then_inc(chunk_out, 1)
                    if layer == 0:
                        neg = net.const[:, CCOL["na_neg"]:CCOL["na_neg"] + GRID_W].unsqueeze(1).to_broadcast([P, 8, GRID_W])
                        for n in range(B_STEPS):
                            dve.wait_ge(b_mm, n + 1)
                            dve.scalar_tensor_tensor(table[:, 8 * n:8 * n + 8, :], ps_b[n % 2][:].rearrange("p (r c) -> p r c", r=8),
                                                     1.0 / SCALE, neg, ALU.mult, ALU.add).then_inc(b_done, 1)
                bias = param(net, "b_mod", 0, DEPTH * 6 * KD).rearrange("p (l j o) -> p l j o", l=DEPTH, o=1)
                vectors = ps_mod[0][:].rearrange("p (l n) -> p l n", n=P)[:, 0:DEPTH, 0:MROWS].rearrange("p l (s j) -> p l j s", s=2)
                dve.wait_ge(mod_t, 1)
                dve.tensor_tensor(mod[:], vectors, bias.to_broadcast([P, DEPTH, 6 * KD, 2]), ALU.add).then_inc(derived, 1)
                dve.wait_ge(derived, 1)
                for layer in range(DEPTH):
                    for site, pre in enumerate(("g_mix_pre", "g_ffn_pre")):
                        part = [mod[:, layer, (3 * site + n) * KD:(3 * site + n + 1) * KD, :] for n in range(2)]
                        gain = param(net, pre, layer * KD, KD).unsqueeze(2).to_broadcast([P, KD, 2])
                        dve.tensor_copy(net.shift[:, layer, site], part[0]).then_inc(derived, 1)
                        dve.scalar_tensor_tensor(net.scale[:, layer, site], part[1], 1.0, gain, ALU.add, ALU.mult).then_inc(derived, 1)
                    taps = param(net, "conv_w", layer * 3 * 2 * FT, 3 * 2 * FT).rearrange("p (t f) -> p f t", t=3)
                    dve.tensor_copy(net.conv[:, layer, :, 0:3], taps).then_inc(derived, 1)
                    dve.tensor_copy(net.conv[:, layer, :, 3], param(net, "conv_b", layer * 2 * FT, 2 * FT)).then_inc(derived, 1)
                dve.wait_ge(derived, 1 + DEPTH * 6)


def project_stage(nc, net, name, layer, site, tiles, weights, out_T, kind, pairs, tail=None, normed=True, early=None):
    NT = len(tiles)
    T = NT * P
    early = early or T
    segs = [(s, min(s + 512, T)) for s in range(0, T, 512)]
    streams = [(0, LAT, 0)] + ([(LAT, T, 1)] if T > LAT else [])
    w_view = weights.rearrange("(k p) n -> p k n", p=P)
    bodies, odd = divmod(pairs, 2)
    assert early == T or SWA_HEADS * HEAD == (pairs - 2) * 2 * P
    assert odd == 0
    HI, LO = "hi", "lo"
    with ExitStack() as ctx:
        sb, pb, sem = sbuf(nc, ctx), psum(nc, ctx), sems(nc, net, ctx, name)
        h_hi, h_lo = (sb(f"{name}_h_{x}", [P, KD, T], F32R) for x in (HI, LO))
        raw = [sb(f"{name}_w_raw{s}", [P, KD, 2 * P]) for s in range(2)]
        w_hi, w_lo = ([sb(f"{name}_w_{x}{s}", [P, KD, 2 * P], F32R) for s in range(2)] for x in (HI, LO))
        region = net.region
        xt = region[:, 0:NT * D].rearrange("p (t d) -> p t d", t=NT)
        buf = [region[:, n * TOK:n * TOK + T] for n in range(8)]
        hf = [sb(f"{name}_hf{s}", [P, 512]) for s in range(2)]
        stat = sb(f"{name}_stat", [P, 3, NT])
        tap = [sb(f"{name}_tap{s}", [P, 2, 4]) for s in range(2)]
        ps = [pb(f"{name}_ps{r}", [P, 3 * 512]) for r in range(2)]
        ps_t = [pb(f"{name}_ps_t{r}", [P, 512]) for r in range(2)]
        x_in = [sem(f"x_in{g}") for g in range(len(segs))]
        w_in = [sem(f"w_in{s}") for s in range(2)]
        sq, ms, rstd, hn, tr, mod1, h_ready = (sem(n) for n in ("sq", "ms", "rstd", "hn", "tr", "mod1", "h_ready"))
        whi, wlo, mm, conv1, act_gate, dve_step, out_ready, taps = (sem(n) for n in (
            "whi", "wlo", "mm", "conv1", "act_gate", "dve_step", "out_ready", "taps"))
        evac = [sem(f"evac{r}") for r in range(2)]
        stored = [sem(f"stored{n}") for n in range(2 if kind == "ffn" else 4)]
        STEPS = 4 * len(streams) + 1

        def cols(i, s):
            if kind == "ffn":
                return [(0, P, ds(i * (2 * P) + s * P, P)), (P, 2 * P, ds(i * (2 * P) + (s * P + DFF), P))]
            return [(0, 2 * P, ds(i * (4 * P) + s * 2 * P, 2 * P))]

        n_in = 32 if kind == "ffn" else 16

        with nc.Block() as block:
            @block.sync
            def _(sp):
                def load(i, s):
                    for a, b, src in cols(i, s):
                        sp.dma_start(raw[s][:, :, a:b], w_view[:, :, src]).then_inc(w_in[s], 16)

                def store(i, s, n=T):
                    if kind == "ffn":
                        sp.wait_ge(out_ready, i * 2 + s + 1)
                        sp.dma_start(out_T[ds(i * (2 * P) + s * P, P), 0:T], buf[4 + s]).then_inc(stored[s], 16)
                    else:
                        for r in range(2):
                            sp.wait_ge(evac[r], i * 2 + (s + 2))
                            sp.dma_start(out_T[ds(i * (4 * P) + (2 * s + r) * P, P), 0:n], buf[2 * s + r][:, 0:n])\
                              .then_inc(stored[2 * s + r], 16)

                for done in stored:
                    sp.sem_inc(done, 16)
                for t in range(NT):
                    if not normed:
                        sp.dma_start(xt[:, t, :], tiles[t]).then_inc(x_in[t // 4], 16)
                    if t in (3, 7):
                        load(0, t // 4)
                with sp.Fori(0, bodies - 1) as b:
                    for s in range(2):
                        sp.wait_ge(wlo, b * 2 + (s + 1))
                        load(b + 1, s)
                        store(b, s, early)
                if tail:
                    sp.wait_ge(wlo, 2 * bodies - 1)
                    sp.dma_start(raw[0][:, :, 0:P], w_view[:, :, tail[0]:tail[0] + P]).then_inc(w_in[0], 16)
                for s in range(2):
                    store(bodies - 1, s)
                if tail:
                    sp.wait_ge(evac[0], 1 + pairs + 1)
                    rows = tail[0] + P - tail[1]
                    sp.dma_start(out_T[tail[1]:tail[1] + rows, 0:T], buf[0][P - rows:P, :]).then_inc(stored[0], 16)
                for n, done in enumerate(stored):
                    sp.wait_ge(done, 16 * (1 + bodies + (bool(tail) and n == 0)))

            @block.scalar
            def _(act):
                def square(g, t):
                    a, b = segs[g]
                    n = D // (b - a)
                    if t == a // P:
                        act.wait_ge(x_in[g], 16 * (b - a) // P)
                    if t:
                        act.wait_ge(sq, t)
                    act.activation(h_lo[:, KD - n:KD, a:b], xt[:, t, :].rearrange("p (n c) -> p n c", n=n), ACT.Square,
                                   accum_out=stat[:, 0, t:t + 1]).then_inc(sq, 1)

                if kind == "plain":
                    act.sem_inc(evac[0], 1)

                def modulate(g):
                    later = list(range(segs[g + 1][0] // P, segs[g + 1][1] // P)) if g + 1 < len(segs) and not normed else []
                    a, b = segs[g]
                    stream = int(a >= LAT)
                    for c in range(KD):
                        u = g * KD + c
                        act.wait_ge(tr, u + 1)
                        if u >= 2:
                            act.wait_ge(h_ready, 2 * (u - 1))
                        act.activation(hf[u % 2][:, 0:b - a], ps_t[u % 2][:, 0:b - a], ACT.Identity,
                                       scale=net.scale[:, layer, site, c, stream:stream + 1],
                                       bias=net.shift[:, layer, site, c, stream:stream + 1]).then_inc(mod1, 1)
                        if c % 2 and later:
                            square(g + 1, later.pop(0))
                        if normed and g == 0 and c == 2:
                            high_part()

                def split(i, s, width=2 * P):
                    act.wait_ge(w_in[s], i * n_in + n_in)
                    act.wait_ge(mm, i * 4 + (2 * s + 2))
                    act.activation(w_hi[s][:, :, 0:width], raw[s][:, :, 0:width], ACT.Copy).then_inc(whi, 1)

                def evacuate(i, s, n=T):
                    if kind == "ffn":
                        act.wait_ge(taps, i * 2 + s + 1)
                        act.wait_ge(dve_step, i * (2 * STEPS) + ((s + 1) * STEPS))
                        for r in range(2):
                            act.wait_ge(mm, i * 4 + (2 * s + r + 5))
                            act.activation(buf[2 * s + r], ps[r][:, 0:T], ACT.Identity, scale=tap[s][:, r, 1:2],
                                           bias=tap[s][:, r, 3:4]).then_inc(conv1, 1)
                        act.wait_ge(dve_step, i * (2 * STEPS) + (2 * STEPS + s * STEPS + 2 * len(streams)))
                        act.activation(buf[6 + s], buf[2 * s], ACT.Silu).then_inc(act_gate, 1)
                    else:
                        act.wait_ge(mm, i * 4 + (2 * s + 5))
                        act.wait_ge(stored[2 * s], i * 16 + 16)
                        act.activation(buf[2 * s][:, 0:n], ps[0][:, 0:n], ACT.Copy).then_inc(evac[0], 1)

                def high_part():
                    act.wait_ge(w_in[0], n_in)
                    act.activation(w_hi[0][:], raw[0][:], ACT.Copy).then_inc(whi, 1)

                if not normed:
                    for t in range(4):
                        square(0, t)
                    high_part()
                for g in range(len(segs)):
                    modulate(g)
                with act.Fori(0, bodies - 1) as b:
                    split(b, 1)
                    evacuate(b, 0, early)
                    split(b + 1, 0)
                    evacuate(b, 1, early)
                split(bodies - 1, 1)
                evacuate(bodies - 1, 0)
                if tail:
                    act.wait_ge(w_in[0], 16 * (bodies + 1))
                    act.wait_ge(mm, 4 * bodies + 2)
                    act.activation(w_hi[0][:, :, 0:P], raw[0][:, :, 0:P], ACT.Copy).then_inc(whi, 1)
                evacuate(bodies - 1, 1)
                if tail:
                    act.wait_ge(mm, 4 + 2 * pairs + 1)
                    act.wait_ge(stored[0], 16 * (bodies + 1))
                    act.activation(buf[0], ps[0][:, 0:T], ACT.Copy).then_inc(evac[0], 1)

            @block.gpsimd
            def _(pool):
                clear_last_stage(pool, net)
                for g, (a, b) in enumerate(segs):
                    t0, t1 = a // P, b // P
                    if not normed:
                        pool.wait_ge(ms, g + 1)
                        pool.tensor_tensor(stat[:, 2, t0:t1], stat[:, 1, t0:t1], net.half[:, 0:t1 - t0], ALU.pow).then_inc(rstd, 1)
                    if not g:
                        pool.wait_ge(whi, 1)
                        pool.tensor_tensor(w_lo[0][:], raw[0][:], w_hi[0][:].bitcast(F32), ALU.subtract).then_inc(wlo, 1)

            @block.vector
            def _(dve):
                dve.sem_inc(dve_step, 2 * STEPS)
                for done in (evac if kind == "ffn" else evac[1:]):
                    dve.sem_inc(done, 1)
                for g, (a, b) in enumerate(segs):
                    t0, t1 = a // P, b // P
                    if not normed:
                        dve.wait_ge(sq, t1)
                        dve.tensor_scalar(stat[:, 1, t0:t1], stat[:, 0, t0:t1], 1.0 / D, EPS, ALU.mult, ALU.add).then_inc(ms, 1)
                        dve.wait_ge(rstd, g + 1)
                        for t in range(t0, t1):
                            dve.tensor_scalar(xt[:, t, :], xt[:, t, :], stat[:, 2, t:t + 1], None, ALU.mult).then_inc(hn, 1)
                    for c in range(KD):
                        u = g * KD + c
                        dve.wait_ge(mod1, u + 1)
                        dve.tensor_copy(h_hi[:, c, a:b], hf[u % 2][:, 0:b - a]).then_inc(h_ready, 1)
                        dve.wait_ge(h_ready, 2 * u + 1)
                        dve.tensor_tensor(h_lo[:, c, a:b], hf[u % 2][:, 0:b - a], h_hi[:, c, a:b].bitcast(F32), ALU.subtract)\
                           .then_inc(h_ready, 1)

                def split(i, s, width=2 * P):
                    dve.wait_ge(whi, i * 2 + s + 1)
                    dve.tensor_tensor(w_lo[s][:, :, 0:width], raw[s][:, :, 0:width], w_hi[s][:, :, 0:width].bitcast(F32),
                                      ALU.subtract).then_inc(wlo, 1)

                def evacuate(i, s, n=T):
                    if kind == "ffn":
                        base = 2 * STEPS + s * STEPS
                        step = 0
                        for r in range(2):
                            dve.wait_ge(conv1, i * 4 + (2 * s + r + 1))
                            for tapn, shift in ((0, -1), (2, 1)):
                                for lo, hi, _ in streams:
                                    dst = buf[2 * s + r][:, max(lo - shift, lo):min(hi - shift, hi)]
                                    src = ps[r][:, max(lo + shift, lo):min(hi + shift, hi)]
                                    last = tapn == 2 and hi == T
                                    o = dve.scalar_tensor_tensor(dst, src, tap[s][:, r, tapn:tapn + 1], dst, ALU.mult, ALU.add)
                                    o.then_inc(dve_step, 1)
                                    step += 1
                                    dve.wait_ge(dve_step, i * (2 * STEPS) + (base + step))
                            dve.sem_inc(evac[r], 1)
                        dve.wait_ge(act_gate, i * 2 + s + 1)
                        dve.wait_ge(stored[s], i * 16 + 16)
                        dve.tensor_tensor(buf[4 + s], buf[6 + s], buf[2 * s + 1], ALU.mult).then_inc(out_ready, 1)
                        dve.wait_ge(out_ready, i * 2 + s + 1)
                        dve.sem_inc(dve_step, 1)
                    else:
                        dve.wait_ge(mm, i * 4 + (2 * s + 6))
                        dve.wait_ge(stored[2 * s + 1], i * 16 + 16)
                        dve.tensor_copy(buf[2 * s + 1][:, 0:n], ps[1][:, 0:n]).then_inc(evac[1], 1)

                def load_taps(i, s):
                    src = net.conv[:, layer].rearrange("p (r f) n -> p r f n", r=2)[:, :, ds(i * 2 + s, 1), :]
                    dve.tensor_scalar(tap[s][:].unsqueeze(2), src, 1.0, None, ALU.mult).then_inc(taps, 1)

                if kind == "ffn":
                    load_taps(0, 0)
                with dve.Fori(0, bodies - 1) as b:
                    if kind == "ffn":
                        load_taps(b, 1)
                    split(b, 1)
                    evacuate(b, 0, early)
                    if kind == "ffn":
                        load_taps(b + 1, 0)
                    split(b + 1, 0)
                    evacuate(b, 1, early)
                if kind == "ffn":
                    load_taps(bodies - 1, 1)
                split(bodies - 1, 1)
                evacuate(bodies - 1, 0)
                if tail:
                    dve.wait_ge(whi, pairs + 1)
                    dve.tensor_tensor(w_lo[0][:, :, 0:P], raw[0][:, :, 0:P], w_hi[0][:, :, 0:P].bitcast(F32),
                                      ALU.subtract).then_inc(wlo, 1)
                evacuate(bodies - 1, 1)

            @block.tensor
            def _(pe):
                pe.sem_inc(mm, 4)

                def turn(g, c):
                    a, b = segs[g]
                    u = g * KD + c
                    if not normed:
                        pe.wait_ge(hn, b // P)
                    if u >= 2:
                        pe.wait_ge(mod1, u - 1)
                    for t in range(a // P, b // P):
                        m = pe.transpose(ps_t[u % 2][:, t * P - a:t * P - a + P], xt[:, t, c * P:(c + 1) * P], net.ident)
                    m.then_inc(tr, 1)

                def product(s, r, width, tokens=T):
                    n = 0
                    for k in range(KD):
                        for w, h in ((w_hi, h_hi), (w_hi, h_lo), (w_lo, h_hi)):
                            for a, b in segs:
                                if a < tokens:
                                    m = pe.matmul(ps[r][:, a:b], w[s][:, k, r * P:(r + 1) * P], h[:, k, a:b],
                                                  start=(n == 0), stop=(n == 3 * KD - 1))
                            n += 1
                    m.then_inc(mm, 1)

                def pair(b, s, tokens):
                    pe.wait_ge(wlo, b * 2 + s + 1)
                    for r in range(2):
                        pe.wait_ge(evac[r], b * 2 + (s + 1))
                        product(s, r, P, tokens)

                for c in range(KD):
                    turn(0, c)
                pe.wait_ge(wlo, 1)
                for g, (a, b) in enumerate(segs):
                    if a >= early:
                        break
                    pe.wait_ge(h_ready, 2 * KD * (g + 1))
                    for r in range(2):
                        for k in range(KD):
                            c = r * KD + k - (0 if normed else 5)
                            if g + 1 < len(segs) and 0 <= c < KD:
                                turn(g + 1, c)
                            for n, (w, h) in enumerate(((w_hi, h_hi), (w_hi, h_lo), (w_lo, h_hi))):
                                m = pe.matmul(ps[r][:, a:b], w[0][:, k, r * P:(r + 1) * P], h[:, k, a:b],
                                              start=(k == 0 and n == 0), stop=(k == KD - 1 and n == 2))
                        if b == early:
                            m.then_inc(mm, 1)
                pair(0, 1, early)
                with pe.Fori(1, bodies - 1) as b:
                    for s in range(2):
                        pair(b, s, early)
                pe.wait_ge(h_ready, 2 * KD * len(segs))
                for s in range(2):
                    pair(bodies - 1, s, T)
                if tail:
                    pe.wait_ge(wlo, pairs + 1)
                    pe.wait_ge(evac[0], pairs + 1)
                    product(0, 0, P)


def close_stage(nc, net, name, layer, site, src_T, weights, width, x_tiles, out_tiles, norm_out=True):
    NT = len(x_tiles)
    groups = [(g, min(g + 4, NT)) for g in range(0, NT, 4)]
    steps = width // (2 * P)
    w_view = weights.rearrange("(j k p) n -> j p k n", p=P, k=2)
    s_view = src_T.rearrange("(j k p) t -> j p k t", p=P, k=2)
    streams = 1 if NT == LAT_TILES else 2
    with ExitStack() as ctx:
        sb, pb, sem = sbuf(nc, ctx), psum(nc, ctx), sems(nc, net, ctx, name)
        w_raw = [sb(f"{name}_w_raw{s}", [P, 2, D]) for s in range(2)]
        w_hi, w_lo = ([sb(f"{name}_w_{x}{s}", [P, 2, D], F32R) for s in range(2)] for x in ("hi", "lo"))
        a_raw = [sb(f"{name}_a_raw{s}", [P, 2, 512]) for s in range(2)]
        a_hi, a_lo = ([sb(f"{name}_a_{x}{s}", [P, 2, 512], F32R) for s in range(2)] for x in ("hi", "lo"))
        gate = sb(f"{name}_gate", [P, 2, D])
        gate_row = sb(f"{name}_gate_row", [P, 2, D])
        xt = sb(f"{name}_xt", [P, 4, D])
        YS = 4
        yt = sb(f"{name}_yt", [P, YS, D])
        sqb = sb(f"{name}_sqb", [P, 2, D])
        stat = sb(f"{name}_stat", [P, 4, NT])
        ROOT = D ** -0.5
        assert ROOT == 1 / 32
        normed = net.region[:, 0:NT * D].rearrange("p (t d) -> p t d", t=NT) if norm_out else None
        ps = [pb(f"{name}_ps{m}", [P, D]) for m in range(4)]
        ld = [sem(f"ld{s}") for s in range(2)]
        (hi, lo, lo_a, mm, y_done, gate_in, gate_set, x_in, sq, rstd, scaled, added, sq2, rstd2, hn, eps) = (sem(n) for n in (
            "hi", "lo", "lo_a", "mm", "y_done", "gate_in", "gate_set", "x_in", "sq", "rstd", "scaled", "added",
            "sq2", "rstd2", "hn", "eps"))
        stored = net.tile_stored
        base = [16 * n for n in net.tiles_stored]
        for t in range(NT):
            net.tiles_stored[t % YS] += 1
        whole = (steps - 3) // 2

        def early_step(g, j, step):
            step(g * steps + j, 0, (g * steps + j) % 2, j == 0, False)

        def other_steps(eng, g, step):
            J = g * steps
            if whole > 0:
                with eng.Fori(0, whole) as b:
                    for s in range(2):
                        step(J + 2 + s, b, (J + s) % 2, False, False)
            for j in range(2 + 2 * whole, steps):
                step(J + j, 0, (J + j) % 2, False, j == steps - 1)

        def run_groups(eng, step, epilogue_of):
            early_step(0, 0, step)
            early_step(0, 1, step)
            for g in range(len(groups)):
                other_steps(eng, g, step)
                more = g + 1 < len(groups)
                if more:
                    early_step(g + 1, 0, step)
                epilogue_of(g, (lambda: early_step(g + 1, 1, step)) if more else (lambda: None))

        def epilogue(g, tile, after, between):
            t0, t1 = groups[g]
            for t in range(t0, t1):
                tile(t)
                if norm_out and t > t0:
                    after(t - 1)
            between()
            if norm_out:
                after(t1 - 1)

        with nc.Block() as block:
            @block.sync
            def _(sp):
                for g, (t0, t1) in enumerate(groups):
                    def load(J, b, s, first, last):
                        if last and not J // steps:
                            own = slice((3 * site + 2) * D, (3 * site + 3) * D)
                            gain = (net.g_mix_post, net.g_ffn_post)[site]
                            rows = [(gate[:, n, :], net.mod_d[layer, n:n + 1, own]) for n in range(streams)]
                            rows += [(gate_row[:, 0, :], net.b_mod[layer:layer + 1, own]), (gate_row[:, 1, :], gain[layer:layer + 1, :])]
                            for dst, row in rows:
                                sp.dma_start(dst, row.to_broadcast([P, D])).then_inc(gate_in, 16)
                        sp.wait_ge(lo, b * 2 + (J + 1))
                        sp.wait_ge(lo_a, b * 2 + (J + 1))
                        sp.dma_start(w_raw[s][:], w_view[b * 2 + (J - g * steps)]).then_inc(ld[s], 16)
                        sp.dma_start(a_raw[s][:, :, 0:(t1 - t0) * P], s_view[b * 2 + (J - g * steps), :, :, t0 * P:t1 * P])\
                          .then_inc(ld[s], 16)
                    early_step(g, 0, load)
                    early_step(g, 1, load)
                    other_steps(sp, g, load)
                    if g:
                        sp.wait_ge(added, t0)
                    for t in range(t0, t1):
                        sp.dma_start(xt[:, t - t0, :], x_tiles[t]).then_inc(x_in, 16)

            @block.gpsimd
            def _(pool):
                clear_last_stage(pool, net)

                pool.sem_inc(lo_a, 2)

                def split(J, b, s, first, last):
                    n = (groups[J // steps][1] - groups[J // steps][0]) * P
                    pool.wait_ge(hi, b * 4 + (2 * J + 1))
                    pool.tensor_tensor(a_lo[s][:, :, 0:n], a_raw[s][:, :, 0:n], a_hi[s][:, :, 0:n].bitcast(F32),
                                       ALU.subtract).then_inc(lo_a, 1)

                roots = [0]

                def inverse_root(n, t, done):
                    roots[0] += 1
                    pool.tensor_scalar(stat[:, n, t:t + 1], stat[:, n, t:t + 1], EPS, None, ALU.add).then_inc(eps, 1)
                    pool.wait_ge(eps, roots[0])
                    pool.tensor_tensor(stat[:, n + 1, t:t + 1], stat[:, n, t:t + 1], net.half[:, 0:1], ALU.pow).then_inc(done, 1)

                def root(t):
                    pool.wait_ge(sq, t + 1)
                    inverse_root(0, t, rstd)
                    if not norm_out:
                        store(t - 1)

                def root2(t):
                    pool.wait_ge(sq2, t + 1)
                    inverse_root(2, t, rstd2)
                    store(t)

                def store(t):
                    if t >= 0:
                        pool.wait_ge(added, t + 1)
                        pool.dma_start(out_tiles[t], yt[:, t % YS, :]).then_inc(stored[t % YS], 16)

                run_groups(pool, split, lambda g, between: epilogue(g, root, root2, between))
                if not norm_out:
                    store(NT - 1)
                for n in range(YS):
                    pool.wait_ge(stored[n], 16 * net.tiles_stored[n])

            @block.scalar
            def _(act):
                def split(J, b, s, first, last):
                    n = (groups[J // steps][1] - groups[J // steps][0]) * P
                    act.wait_ge(ld[s], b * 32 + 32 * (J // 2 + 1))
                    act.wait_ge(mm, b * 2 + J + 1)
                    act.activation(a_hi[s][:, :, 0:n], a_raw[s][:, :, 0:n], ACT.Copy).then_inc(hi, 1)
                    act.activation(w_hi[s][:], w_raw[s][:], ACT.Copy).then_inc(hi, 1)

                def square(t):
                    act.wait_ge(y_done, t + 1)
                    if t:
                        act.wait_ge(sq, t)
                    act.activation(sqb[:, 0, :], ps[t % 4][:], ACT.Square, scale=ROOT, accum_out=stat[:, 0, t:t + 1]).then_inc(sq, 1)

                def square2(t):
                    act.wait_ge(added, t + 1)
                    if t:
                        act.wait_ge(sq2, t)
                    act.activation(sqb[:, 1, :], yt[:, t % YS, :], ACT.Square, scale=ROOT, accum_out=stat[:, 2, t:t + 1]).then_inc(sq2, 1)

                run_groups(act, split, lambda g, between: epilogue(g, square, square2, between))

            @block.vector
            def _(dve):
                dve.sem_inc(lo, 2)

                def split(J, b, s, first, last):
                    dve.wait_ge(hi, b * 4 + (2 * J + 2))
                    dve.tensor_tensor(w_lo[s][:], w_raw[s][:], w_hi[s][:].bitcast(F32), ALU.subtract).then_inc(lo, 1)
                    if last and J < steps:
                        dve.wait_ge(gate_in, 16 * (streams + 2))
                        row = [gate_row[:, n, :].unsqueeze(1).to_broadcast([P, streams, D]) for n in range(2)]
                        dve.tensor_tensor(gate[:, 0:streams, :], gate[:, 0:streams, :], row[0], ALU.add).then_inc(gate_set, 1)
                        dve.wait_ge(gate_set, 1)
                        dve.tensor_tensor(gate[:, 0:streams, :], gate[:, 0:streams, :], row[1], ALU.mult).then_inc(gate_set, 1)

                def tile(t):
                    y = yt[:, t % YS, :]
                    dve.wait_ge(gate_set, 2)
                    dve.wait_ge(rstd, t + 1)
                    if t >= YS:
                        dve.wait_ge(stored[t % YS], base[t % YS] + 16 * (t // YS))
                    dve.scalar_tensor_tensor(y, ps[t % 4][:], stat[:, 1, t:t + 1], gate[:, int(t >= LAT_TILES), :],
                                             ALU.mult, ALU.mult).then_inc(scaled, 1)
                    dve.wait_ge(scaled, t + 1)
                    dve.wait_ge(x_in, 16 * min(NT, t // 4 * 4 + 4))
                    dve.tensor_tensor(y, y, xt[:, t % 4, :], ALU.add).then_inc(added, 1)

                def normalise(t):
                    dve.wait_ge(rstd2, t + 1)
                    dve.tensor_scalar(normed[:, t, :], yt[:, t % YS, :], stat[:, 3, t:t + 1], None, ALU.mult).then_inc(hn, 1)

                run_groups(dve, split, lambda g, between: epilogue(g, tile, normalise, between))
                if norm_out:
                    dve.wait_ge(hn, NT)

            @block.tensor
            def _(pe):
                pe.sem_inc(mm, 2)
                for g, (t0, t1) in enumerate(groups):
                    PASSES = ((a_hi, w_hi), (a_hi, w_lo), (a_lo, w_hi))

                    def one(s, m_, kk, n, first, last):
                        a, w = PASSES[n]
                        for half in range(2):
                            m = pe.matmul(ps[m_][:, half * 512:(half + 1) * 512], a[s][:, kk, m_ * P:(m_ + 1) * P],
                                          w[s][:, kk, half * 512:(half + 1) * 512],
                                          start=(first and kk == 0 and n == 0), stop=(last and kk == 1 and n == 2))
                        return m

                    def multiply(J, b, s, first, last):
                        if J == 0:
                            pe.wait_ge(hi, 2)
                            for n in range(3):
                                if n == 1:
                                    pe.wait_ge(lo, 3)
                                    pe.wait_ge(lo_a, 3)
                                for m_ in range(t1 - t0):
                                    for kk in range(2):
                                        m = one(s, m_, kk, n, first, last)
                            m.then_inc(mm, 1)
                            return
                        pe.wait_ge(lo, b * 2 + (J + 1 + 2))
                        pe.wait_ge(lo_a, b * 2 + (J + 1 + 2))
                        for m_ in range(t1 - t0):
                            if first and g:
                                pe.wait_ge(scaled, (t0 - 4) + m_ + 1)
                            for kk in range(2):
                                for n in range(3):
                                    m = one(s, m_, kk, n, first, last)
                            if last:
                                m.then_inc(y_done, 1)
                        if last:
                            pe.wait_ge(y_done, t1)
                            pe.sem_inc(mm, 1)
                        else:
                            m.then_inc(mm, 1)
                    early_step(g, 0, multiply)
                    early_step(g, 1, multiply)
                    other_steps(pe, g, multiply)


def attention_stage(nc, net, name, proj, y_T, banded):
    GROUPS = KV if banded else NA_HEADS // 2
    BODIES = GROUPS // 2
    CHUNKS = 2 if banded else 1
    T_OUT = LAT if banded else TOK
    HALF = P // 2
    with ExitStack() as ctx:
        sb, pb, sem = sbuf(nc, ctx), psum(nc, ctx), sems(nc, net, ctx, name)
        q = [sb(f"{name}_q{r}", [P, CHUNKS, T_OUT]) for r in range(2)]
        k = [sb(f"{name}_k{r}", [P, TOK]) for r in range(2)]
        q_hi, q_lo = ([sb(f"{name}_q_{x}{r}", [P, CHUNKS, T_OUT], F32R) for r in range(2)] for x in ("hi", "lo"))
        k_hi, k_lo = ([sb(f"{name}_k_{x}{r}", [P, 2, TOK], F32R) for r in range(2)] for x in ("hi", "lo"))
        if banded:
            vt_rows = [slice(r * HALF, (r + 1) * HALF) for r in range(2)]
            vt = [sb(f"{name}_vt", [P, TOK])] * 2
        else:
            vt_rows = [slice(0, P)] * 2
            vt = [sb(f"{name}_vt{r}", [P, TOK]) for r in range(2)]
        v = [sb(f"{name}_v{r}", [P, TOK // P, P]) for r in range(2)]
        yt = [sb(f"{name}_yt{r}", [P, CHUNKS, T_OUT]) for r in range(2)]
        yb = [sb(f"{name}_yb{n}", [P, CHUNKS * P]) for n in range(2)]
        prob = [sb(f"{name}_prob{n}", [P, 832]) for n in range(2)]
        pt = [sb(f"{name}_pt{n}", [P, 7 * P]) for n in range(2)]
        mx = sb(f"{name}_mx", [P, 3, 2])
        den = sb(f"{name}_den", [P, 4, 5])
        if banded:
            q_sw = [sb(f"{name}_q_sw{r}", [P, CHUNKS, LAT]) for r in range(2)]
            k_sw = [sb(f"{name}_k_sw{r}", [P, LAT]) for r in range(2)]
            rope = sb(f"{name}_rope", [P, 2, LAT])
            sink_all = sb(f"{name}_sink_all", [P, SWA_HEADS])
            sink8 = [sb(f"{name}_sink8{r}", [P, GROUP]) for r in range(2)]
        else:
            bias = [sb(f"{name}_bias{r}", [P, 2, BIAS_COLS]) for r in range(2)]
        ps_s = [pb(f"{name}_ps_s{n}", [P, 1024]) for n in range(2)]
        ps_p = pb(f"{name}_ps_p", [P, 1024])
        ps_o = pb(f"{name}_ps_o", [P, 512])
        ps_y = pb(f"{name}_ps_y", [P, 512])
        ld = [sem(f"ld{r}") for r in range(2)]
        stored = [sem(f"stored{r}") for r in range(2)]
        held, turning, padded, v_padded = (sem(n) for n in ("held", "turning", "padded", "v_padded"))
        rotated_first, hi_first, split_first, parted = (sem(n) for n in ("rotated_first", "hi_first", "split_first", "parted"))
        zero_set = sem("zero_set")
        (scores, front, maxed, probs, trans, pt_a, pt_b, out_mm, recip, normed, y_tr, y_ev, v_tr, v_ev, zeroed,
         rotated, rope_in, sinks) = (sem(n) for n in (
             "scores", "front", "maxed", "probs", "trans", "pt_a", "pt_b", "out_mm", "recip", "normed", "y_tr", "y_ev",
             "v_tr", "v_ev", "zeroed", "rotated", "rope_in", "sinks"))

        def unit(r, tile, head):
            if banded:
                chunk, half, vcol = head // 2, head % 2, 0
            else:
                chunk, half, vcol = 0, head, head * HEAD
            u = {"r": r, "vcol": vcol, "q": tuple(x[r][:, chunk, tile * P:(tile + 1) * P] for x in (q_hi, q_lo)),
                 "head": head}
            if tile >= LAT_TILES:
                lat, u["bias"] = (0, 0), None
            elif banded:
                lat = (max(tile - 1, 0) * P, min(tile + 2, LAT_TILES) * P)
                c0 = CCOL["swa_mask"] + (P if tile == 0 else 0)
                u["bias"] = net.const[:, c0:c0 + lat[1] - lat[0]]
            else:
                first, second = (min(max(row - NA_ROWS // 2, 0), LAT // GRID_W - NA_ROWS) for row in (2 * tile, 2 * tile + 1))
                inner = first != second
                n = (NA_ROWS + 1) if inner else NA_ROWS
                lat = (first * GRID_W, (first + n) * GRID_W)
                slot = EDGE_SLOTS if inner else first - 2 * tile + NA_ROWS - 1
                u["bias"] = bias[r][:, head, slot * GRID_W:(slot + n) * GRID_W]
            keys, blocks = [], []
            at = packed = 0
            for a, b in (lat, (LAT, TOK)):
                done = a
                if a == LAT and banded and at % 512:
                    at = 512
                start = at
                while done < b:
                    n = min(b - done, 512 - at % 512)
                    keys.append((at, n, tuple(x[r][:, half, done:done + n] for x in (k_hi, k_lo))))
                    at, done = at + n, done + n
                for t in range(a, b, P):
                    n = min(P, b - t)
                    blocks.append((packed, n, v[r][0:n, t // P, :]))
                    packed += n
            n_lat = lat[1] - lat[0]
            parts = [(0, 0, n_lat + CTXN)] if start == n_lat else [(0, 0, n_lat), (start, n_lat, CTXN)]
            u.update(keys=keys, blocks=blocks, parts=parts, lat=n_lat, ctx=start)
            return u

        heads = GROUP if banded else 2
        tiles = range(T_OUT // P)
        units = [unit(r, tile, head) for r in range(2) for tile in tiles for head in range(heads)]
        U = len(units)
        UG = U // 2
        Y = U // heads
        YG = Y // 2
        front_of = [0]
        for w in units:
            front_of.append(front_of[-1] + (2 if w["bias"] is not None else 1))
        F = front_of[-1]
        V_GROUPS = [(t, min(t + 4, TOK // P)) for t in range(0, TOK // P, 4)]
        VW_ = HEAD if banded else P
        SHARE = 1 if banded else 4
        N_LD = 10 if banded else 4
        SWITCH = UG - 1
        TURNED = (SWITCH - 3) // heads

        def rotations(r):
            ops = [(q[r][:, c, :], q_sw[r][:, c, :], slice(0, P)) for c in range(CHUNKS)]
            return ops + [(k[r][:, 0:LAT], k_sw[r][:], slice(0, P))]
        ROTATED = 3 * (CHUNKS + 1)

        def splits(r):
            halves = [slice(half * HALF, (half + 1) * HALF) for half in range(2)]
            return [(k[r][rows, :], k_hi[r][rows, half, :], k_lo[r][rows, half, :]) for half, rows in enumerate(halves)] + \
                [(q[r][:], q_hi[r][:], q_lo[r][:])]
        SPLITS = 3
        zeros = yt[0][:].rearrange("p c t -> p (c t)")[:, 0:TOK]
        other_halves = lambda x: [x[r][(1 - half) * HALF:(2 - half) * HALF, half, :] for r in range(2) for half in range(2)]

        with nc.Block() as block:
            @block.sync
            def _(sp):
                def load(i, r):
                    g = i * 2 + r
                    inc = lambda d: d.then_inc(ld[r], 16)
                    if banded:
                        qr = proj[ds(i * (2 * GROUP * HEAD) + r * GROUP * HEAD, GROUP * HEAD), :]
                        kr = proj[ds(i * (2 * HEAD) + (SWA_HEADS + r) * HEAD, HEAD), :]
                        vr = proj[ds(i * (2 * HEAD) + (SWA_HEADS + KV + r) * HEAD, HEAD), :]
                        swap = qr.rearrange("(c h two) t -> two h c t", c=2, two=2)
                        kswap = kr.rearrange("(h two) t -> two h t", two=2)
                        inc(sp.dma_start(q[r][:], qr.rearrange("(c p) t -> p c t", c=2)[:, :, 0:LAT]))
                        for two in range(2):
                            inc(sp.dma_start(q_sw[r][two::2], swap[1 - two, :, :, 0:LAT]))
                        for half in range(2):
                            inc(sp.dma_start(k[r][half * HALF:(half + 1) * HALF, :], kr))
                            for two in range(2):
                                inc(sp.dma_start(k_sw[r][half * HALF + two:(half + 1) * HALF:2, :], kswap[1 - two, :, 0:LAT]))
                        inc(sp.dma_start(vt[r][vt_rows[r], :], vr))
                    else:
                        for dst, base in ((k[r][:], NAW), (q[r][:, 0, :], 0), (vt[r][:], 2 * NAW)):
                            inc(sp.dma_start(dst, proj[ds(i * (2 * P) + r * P + base, P), :]))
                        inc(sp.dma_start(bias[r][:], net.bias_d[ds(i * 4 + 2 * r, 2)].rearrange("h p n -> p h n")))

                def store(i, r):
                    sp.wait_ge(y_ev, i * Y + ((r + 1) * YG + 1))
                    rows = y_T[ds(i * (2 * CHUNKS * P) + r * CHUNKS * P, CHUNKS * P), 0:T_OUT]
                    sp.dma_start(rows.rearrange("(c p) t -> p c t", c=CHUNKS), yt[r][:]).then_inc(stored[r], 16)

                for r in range(2):
                    sp.sem_inc(stored[r], 16)
                if banded:
                    sp.dma_start(rope[:], net.rope_d.rearrange("n p t -> p n t")).then_inc(rope_in, 16)
                    sp.dma_start(sink_all[:], net.swa_sink[0:1, :].to_broadcast([P, SWA_HEADS])).then_inc(rope_in, 16)
                for r in range(2):
                    load(0, r)
                with sp.Fori(0, BODIES - 1) as i:
                    for r in range(2):
                        store(i, r)
                        load(i + 1, r)
                for r in range(2):
                    store(BODIES - 1, r)
                for r in range(2):
                    sp.wait_ge(stored[r], 16 * (1 + BODIES))

            @block.gpsimd
            def _(pool):
                clear_last_stage(pool, net)

                def rotate(i, r, ops):
                    n = r * ROTATED
                    for x, xs, rows in ops:
                        cos, sin = (rope[rows, j, :] for j in range(2))
                        pool.tensor_tensor(xs, xs, sin, ALU.mult).then_inc(rotated, 1)
                        pool.tensor_tensor(x, x, cos, ALU.mult).then_inc(rotated, 1)
                        n += 2
                        pool.wait_ge(rotated, i * (2 * ROTATED) + n)
                        pool.tensor_tensor(x, x, xs, ALU.add).then_inc(rotated, 1)
                        n += 1
                        pool.wait_ge(rotated, i * (2 * ROTATED) + n)

                def group(i, r):
                    pool.wait_ge(ld[r], i * (16 * N_LD) + 16 * N_LD)
                    if banded:
                        rotate(i, r, rotations(r))
                    for n, (x, hi, lo) in enumerate(splits(r)):
                        done = 2 * (SPLITS * r + n)
                        pool.tensor_copy(hi, x).then_inc(parted, 1)
                        pool.wait_ge(parted, i * (4 * SPLITS) + (done + 1))
                        pool.tensor_tensor(lo, x, hi.bitcast(F32), ALU.subtract).then_inc(parted, 1)
                        pool.wait_ge(parted, i * (4 * SPLITS) + (done + 2))

                if banded:
                    pool.wait_ge(rope_in, 32)
                    pool.wait_ge(ld[0], 16 * N_LD)
                    rotate(0, 0, rotations(0)[:1])
                    pool.sem_inc(rotated, ROTATED - 3)
                pool.sem_inc(parted, 2 * SPLITS)
                with pool.Fori(0, BODIES - 1) as i:
                    group(i, 1)
                    group(i + 1, 0)
                group(BODIES - 1, 1)

            @block.tensor
            def _(pe):
                pe.sem_inc(trans, 2)
                pe.sem_inc(out_mm, 2)
                pe.sem_inc(y_tr, 2)
                pe.wait_ge(zeroed, 1)
                pe.wait_ge(padded, 8)
                if banded:
                    pe.wait_ge(v_padded, 2)

                def values(i, r):
                    pe.wait_ge(ld[r], i * (16 * N_LD) + 16 * N_LD)
                    pe.wait_ge(y_ev, i * Y + (r * TURNED + 1))
                    for n, (a, b) in enumerate(V_GROUPS):
                        if n:
                            pe.wait_ge(v_ev, i * (2 * len(V_GROUPS)) + (r * len(V_GROUPS) + n))
                        pe.sem_inc(turning, 1)
                        for t in range(a, b):
                            rows = vt_rows[r]
                            m = pe.transpose(ps_y[:, (t - a) * VW_:(t - a + 1) * VW_], vt[r][rows, t * P:(t + 1) * P],
                                             net.ident[rows, rows])
                        m.then_inc(v_tr, 1)
                    pe.wait_ge(v_ev, i * (2 * len(V_GROUPS)) + ((r + 1) * len(V_GROUPS)))

                def score(i, u):
                    w = units[u]
                    if u == 0:
                        pe.wait_ge(split_first, SPLITS)
                    if u % UG == 0:
                        pe.wait_ge(parted, i * (4 * SPLITS) + 2 * SPLITS * (w["r"] + 1))
                    pe.wait_ge(probs, i * U + (u + 1))
                    for at, n, (hi, lo) in w["keys"]:
                        for j, (a, b) in enumerate(((0, hi), (0, lo), (1, hi))):
                            m = pe.matmul(ps_s[u % 2][:, at:at + n], w["q"][a], b, start=(j == 0), stop=(j == 2))
                    m.then_inc(scores, 1)

                def transpose(i, u):
                    w = units[u]
                    pe.wait_ge(pt_a, i * U + (u + 1))
                    pe.wait_ge(pt_b, i * U + (u + 1))
                    pe.wait_ge(probs, i * U + (u + 3))
                    for j, (at, n, _) in enumerate(w["blocks"]):
                        c = j * P if j < SHARE else 512 + (j - SHARE) * P
                        m = pe.transpose(ps_p[0:n, c:c + P], prob[u % 2][:, at:at + n], net.ident)
                    m.then_inc(trans, 1)

                def output(i, u):
                    w = units[u]
                    pe.wait_ge(normed, i * U + (u + 1))
                    pe.wait_ge(pt_a, i * U + (u + 2))
                    pe.wait_ge(pt_b, i * U + (u + 2))
                    last = len(w["blocks"]) - 1
                    for j, (_, n, val) in enumerate(w["blocks"]):
                        m = pe.matmul(ps_o[:, 0:P], pt[u % 2][0:n, j * P:(j + 1) * P], val, start=(j == 0), stop=(j == last))
                    m.then_inc(out_mm, 1)

                def turn(i, y):
                    pe.wait_ge(y_ev, i * Y + (y + 1))
                    pe.wait_ge(normed, i * U + (heads * (y + 1) + 1))
                    for c in range(CHUNKS):
                        m = pe.transpose(ps_y[:, c * P:(c + 1) * P], yb[y % 2][:, c * P:(c + 1) * P], net.ident)
                    m.then_inc(y_tr, 1)

                with pe.Fori(0, BODIES) as i:
                    values(i, 0)
                    score(i, 0)
                    score(i, 1)
                    for u in range(U + 4):
                        if u + 2 < U:
                            score(i, u + 2)
                        if u == SWITCH:
                            values(i, 1)
                        if u < U:
                            transpose(i, u)
                        if 1 <= u <= U:
                            output(i, u - 1)
                        if u >= heads + 2 and (u - 2) % heads == 0 and (u - 2) // heads <= Y:
                            turn(i, (u - 2) // heads - 1)

            @block.scalar
            def _(act):
                act.sem_inc(probs, 2)
                act.sem_inc(pt_b, 1)
                act.sem_inc(y_ev, 1)
                act.wait_ge(zero_set, 1)
                for to in other_halves(k_hi):
                    act.activation(to, zeros[0:HALF], ACT.Copy).then_inc(padded, 1)

                def values(i, r):
                    for n, (a, b) in enumerate(V_GROUPS):
                        act.wait_ge(v_tr, i * (2 * len(V_GROUPS)) + (r * len(V_GROUPS) + n + 1))
                        act.activation(v[r][:, a:b, 0:VW_], ps_y[:, 0:(b - a) * VW_].rearrange("p (t c) -> p t c", c=VW_),
                                       ACT.Copy).then_inc(v_ev, 1)

                def exponentials(i, u):
                    w = units[u]
                    act.wait_ge(trans, i * U + (u + 1))
                    act.wait_ge(maxed, i * U + (u + 1))
                    top = mx[:, 2, u % 2:u % 2 + 1]
                    if banded:
                        act.activation(den[:, u % 4, 0:1], sink8[w["r"]][:, w["head"]:w["head"] + 1], ACT.Exp,
                                       bias=top, scale=SCALE).then_inc(sinks, 1)
                    for j, (src, dst, n) in enumerate(w["parts"]):
                        m = act.activation(prob[u % 2][:, dst:dst + n], ps_s[u % 2][:, src:src + n], ACT.Exp, bias=top,
                                           scale=SCALE, accum_out=den[:, u % 4, 1 + j:2 + j])
                        m.then_inc(probs if j + 1 == len(w["parts"]) else sinks, 1)

                def copy_b(i, u):
                    n = len(units[u]["blocks"])
                    act.wait_ge(out_mm, i * U + (u + 1))
                    act.wait_ge(trans, i * U + (u + 3))
                    if n > SHARE:
                        act.activation(pt[u % 2][:, SHARE * P:n * P], ps_p[:, 512:512 + (n - SHARE) * P], ACT.Copy).then_inc(pt_b, 1)
                    else:
                        act.sem_inc(pt_b, 1)

                def turned(i, y):
                    act.wait_ge(stored[y // YG], i * 16 + 16)
                    act.wait_ge(y_tr, i * Y + (y + 3))
                    t = y % YG
                    act.activation(yt[y // YG][:, :, t * P:(t + 1) * P], ps_y[:, 0:CHUNKS * P].rearrange("p (c t) -> p c t", c=CHUNKS),
                                   ACT.Copy).then_inc(y_ev, 1)

                act.wait_ge(ld[0], 16 * N_LD)
                if banded:
                    act.wait_ge(rotated_first, 6)
                for n, (x, hi, _) in enumerate(splits(0)):
                    if banded and n == 2:
                        act.wait_ge(rotated, 3)
                    act.activation(hi, x, ACT.Copy).then_inc(hi_first, 1)
                with act.Fori(0, BODIES) as i:
                    values(i, 0)
                    for u in range(U + 5):
                        if u < U:
                            exponentials(i, u)
                        if 1 <= u <= U:
                            copy_b(i, u - 1)
                        if u >= heads + 3 and (u - 3) % heads == 0 and (u - 3) // heads <= Y:
                            turned(i, (u - 3) // heads - 1)
                        if u == SWITCH:
                            values(i, 1)

            @block.vector
            def _(dve):
                dve.sem_inc(pt_a, 1)
                dve.sem_inc(normed, 1)
                dve.memset(zeros, 0.0).then_inc(zero_set, 1)
                dve.memset(ps_p[:], 0.0).then_inc(zeroed, 1)
                dve.wait_ge(zero_set, 1)
                for to in other_halves(k_lo):
                    dve.tensor_copy(to, zeros[0:HALF]).then_inc(padded, 1)
                if banded:
                    for r in range(2):
                        dve.memset(v[r][:, :, HEAD:P], 0.0).then_inc(v_padded, 1)
                    dve.wait_ge(rope_in, 32)
                    dve.wait_ge(ld[0], 16 * N_LD)
                    for n, (x, xs, rows) in enumerate(rotations(0)[1:]):
                        cos, sin = (rope[rows, j, :] for j in range(2))
                        dve.tensor_tensor(xs, xs, sin, ALU.mult).then_inc(rotated_first, 1)
                        dve.tensor_tensor(x, x, cos, ALU.mult).then_inc(rotated_first, 1)
                        dve.wait_ge(rotated_first, 3 * n + 2)
                        dve.tensor_tensor(x, x, xs, ALU.add).then_inc(rotated_first, 1)
                    dve.wait_ge(rope_in, 32)
                    dve.tensor_scalar(sink_all[:], sink_all[:], 1.0 / SCALE, None, ALU.mult).then_inc(zeroed, 1)
                    dve.wait_ge(zeroed, 2)

                for n, (x, hi, lo) in enumerate(splits(0)):
                    dve.wait_ge(hi_first, n + 1)
                    dve.tensor_tensor(lo, x, hi.bitcast(F32), ALU.subtract).then_inc(split_first, 1)

                def maximum(i, u):
                    w = units[u]
                    s, lat, c0 = ps_s[u % 2], w["lat"], w["ctx"]
                    row = [mx[:, j, u % 2:u % 2 + 1] for j in range(3)]
                    dve.wait_ge(scores, i * U + (u + 1))
                    dve.reduce_max(row[0], s[:, c0:c0 + CTXN], AX_X).then_inc(front, 1)
                    dve.wait_ge(front, i * F + (front_of[u] + 1))
                    if w["bias"] is not None:
                        dve.sem_inc(held, 1)
                        dve.tensor_tensor_reduce(s[:, 0:lat], s[:, 0:lat], w["bias"], 1.0, row[0], ALU.add, ALU.max, row[1])\
                           .then_inc(front, 1)
                        dve.wait_ge(front, i * F + (front_of[u] + 2))
                        top = row[1]
                    else:
                        top = row[0]
                    if banded:
                        dve.tensor_scalar(row[2], top, sink8[w["r"]][:, w["head"]:w["head"] + 1], -SCALE, ALU.max, ALU.mult)\
                           .then_inc(maxed, 1)
                    else:
                        dve.tensor_scalar(row[2], top, -SCALE, None, ALU.mult).then_inc(maxed, 1)

                def copy_a(i, u):
                    n = min(len(units[u]["blocks"]), SHARE)
                    dve.wait_ge(out_mm, i * U + (u + 1))
                    dve.wait_ge(trans, i * U + (u + 3))
                    dve.tensor_copy(pt[u % 2][:, 0:n * P], ps_p[:, 0:n * P]).then_inc(pt_a, 1)

                R = 2 if banded else 1

                def normalise(i, u):
                    w = units[u]
                    y = u // heads
                    d = [den[:, u % 4, j:j + 1] for j in range(5)]
                    if banded:
                        dve.tensor_reduce(d[3], den[:, u % 4, 0:1 + len(w["parts"])], AX_X, ALU.add).then_inc(recip, 1)
                        dve.wait_ge(recip, i * (R * U) + (R * u + 1))
                    dve.reciprocal(d[4], d[3 if banded else 1]).then_inc(recip, 1)
                    dve.wait_ge(y_tr, i * Y + (y + 1))
                    dve.wait_ge(out_mm, i * U + (u + 3))
                    dve.wait_ge(recip, i * (R * U) + (R * u + R))
                    dve.tensor_scalar(yb[y % 2][:, w["head"] * HEAD:(w["head"] + 1) * HEAD], ps_o[:, w["vcol"]:w["vcol"] + HEAD], d[4], None,
                                      ALU.mult).then_inc(normed, 1)

                def sinks_of(i, r):
                    dve.tensor_scalar(sink8[r][:], sink_all[:, ds(i * (2 * GROUP) + r * GROUP, GROUP)], 1.0, None,
                                      ALU.mult).then_inc(zeroed, 1)
                    dve.wait_ge(zeroed, i * 2 + (3 + r))

                with dve.Fori(0, BODIES) as i:
                    for u in range(-1, U + 2):
                        if banded and (u + 1) % UG == 0 and u + 1 < U:
                            sinks_of(i, (u + 1) // UG)
                        if u + 1 < U:
                            maximum(i, u + 1)
                        if 1 <= u <= U:
                            copy_a(i, u - 1)
                        if u >= 2:
                            normalise(i, u - 2)


def gla_stage(nc, net, name, proj, y_T):
    NT, NCH = TOK // P, TOK // CHUNK
    PAIRS = GLA_HEADS // 2
    base_q, base_k, base_v, base_r, base_z = (3 * NAW, 3 * NAW + KW, 3 * NAW + 2 * KW, 3 * NAW + 2 * KW + VW,
                                              3 * NAW + 2 * KW + 2 * VW)
    segs = [(s, min(s + 512, TOK)) for s in range(0, TOK, 512)]
    order = [list(range(LAT_TILES, NT)) + list(range(LAT_TILES)), list(range(NT - 1, LAT_TILES - 1, -1)) + list(range(LAT_TILES - 1, -1, -1))]
    halves = [(0, 1), (1, 0)]
    hp_rows = [slice(0, DK), slice(DK, 2 * DK)]
    with ExitStack() as ctx:
        sb, pb, sem = sbuf(nc, ctx), psum(nc, ctx), sems(nc, net, ctx, name)
        zt = [sb(f"{name}_zt{d}", [RANK, TOK]) for d in range(2)]
        wa = sb(f"{name}_wa", [RANK, 2, KW])
        qf, kf = sb(f"{name}_q", [P, PAIRS, TOK]), sb(f"{name}_k", [P, PAIRS, TOK])
        vf = sb(f"{name}_vf", [P, GLA_HEADS, TOK])
        kt, kd = (vf[:, n * PAIRS:(n + 1) * PAIRS, :] for n in range(2))
        v = sb(f"{name}_v", [P, NT, VW])
        sr = sb(f"{name}_sr", [P, GLA_HEADS, TOK])
        la = [sb(f"{name}_la{d}", [P, PAIRS, TOK]) for d in range(2)]
        b = sb(f"{name}_b", [P, PAIRS, TOK])
        e = sb(f"{name}_e", [P, PAIRS, TOK])
        qt = sb(f"{name}_qt", [P, PAIRS, TOK])
        kd_tok = sb(f"{name}_kd_tok", [P, NT, KW])
        o = sb(f"{name}_o", [P, NT, VW])
        state = [sb(f"{name}_state{n}", [P, GLA_HEADS, DV]) for n in range(3)]
        att = [sb(f"{name}_att{n}", [P, 2, PAIRS, P]) for n in range(2)]
        dec = sb(f"{name}_dec", [P, PAIRS, NCH])
        seg_mask = [sb(f"{name}_seg{d}", [P, TOK]) for d in range(2)]
        stat = sb(f"{name}_stat", [P, 3, NT, GLA_HEADS])
        junk = sb(f"{name}_junk", [P, DV])
        bank_z = [pb(f"{name}_z{n}", [P, 3 * 512]) for n in range(2)]
        ps_a = [bank_z[1][:, 0:512], bank_z[1][:, 512:1024]]
        ps_d = [bank_z[1][:, 1024:1536], pb(f"{name}_ps_d", [P, 512])[:]]
        ps_o = [pb(f"{name}_ps_o", [P, 512])[:], bank_z[0][:, 0:512]]
        ps_t = [bank_z[0][:, 512:1024], bank_z[0][:, 1024:1536]]
        (z_in, qk_in, v_in, r_in, masks, z_mm, z_abs, z_exp, z_ln, z_min, la_done, silu, gated, v_tr, v_ev, scanned, e1, e2,
         e3, diff, qt_done, kt_done, kd_done, decs, kd_tr, kd_ev, att_mm, att_s, ds_mm, st, st_pe, o_mm, o_ev, o_sum, sq, ms,
         rstd, normed, y_tr, y_ev, stored) = (sem(n) for n in (
             "z_in", "qk_in", "v_in", "r_in", "masks", "z_mm", "z_abs", "z_exp", "z_ln", "z_min", "la_done", "silu",
             "gated", "v_tr", "v_ev", "scanned", "e1", "e2", "e3", "diff", "qt_done", "kt_done", "kd_done", "decs",
             "kd_tr", "kd_ev", "att_mm", "att_s", "ds_mm", "st", "st_pe", "o_mm", "o_ev", "o_sum", "sq", "ms", "rstd",
             "normed", "y_tr", "y_ev", "stored"))
        soft = lambda n: (e, b)[n // PAIRS][:, n % PAIRS, :]
        KG = NT // 2
        chunked = lambda x: x.rearrange("p a (n c) -> p a n c", c=CHUNK)

        def last_of(d):
            edge = CHUNK - 1 if d == 0 else 0
            return chunked(b[:])[:, :, :, edge:edge + 1]

        with nc.Block() as block:
            @block.sync
            def _(sp):
                rows = lambda base, n: proj[base:base + n, :]
                for d in range(2):
                    sp.dma_start(zt[d][:], rows(base_z + d * RANK, RANK)).then_inc(z_in, 16)
                sp.dma_start(wa[:], net.gla_wa2[0].rearrange("d k n -> k d n")).then_inc(z_in, 16)
                sp.dma_start(vf[:], rows(base_v, VW).rearrange("(h p) t -> p h t", p=P)).then_inc(v_in, 16)
                sp.dma_start(qf[:], rows(base_q, KW).rearrange("(h p) t -> p h t", p=P)).then_inc(qk_in, 16)
                sp.dma_start(kf[:], rows(base_k, KW).rearrange("(h p) t -> p h t", p=P)).then_inc(qk_in, 16)
                sp.dma_start(sr[:], rows(base_r, VW).rearrange("(h p) t -> p h t", p=P)).then_inc(r_in, 16)
                out = y_T[NAW:D, :].rearrange("(h p) t -> p h t", p=P)
                cut = LAT_TILES // 2
                sp.wait_ge(y_ev, NT - cut)
                sp.dma_start(out[:, :, cut * P:TOK], sr[:, :, cut * P:TOK]).then_inc(stored, 16)
                sp.wait_ge(y_ev, NT)
                sp.dma_start(out[:, :, 0:cut * P], sr[:, :, 0:cut * P]).then_inc(stored, 16)
                sp.wait_ge(stored, 32)

            @block.gpsimd
            def _(pool):
                clear_last_stage(pool, net)
                for d in range(2):
                    pool.memset(seg_mask[d][:], 1.0).then_inc(masks, 1)
                for n in range(3):
                    pool.memset(state[n][:], 0.0).then_inc(masks, 1)
                pool.wait_ge(masks, 5)
                for d, edge in enumerate((0, CHUNK - 1)):
                    m = seg_mask[d][:].rearrange("p (n c) -> p n c", c=CHUNK)[:, :, edge:edge + 1]
                    pool.memset(m, 0.0).then_inc(masks, 1)
                pool.wait_ge(silu, 1)
                for h in range(GLA_HEADS):
                    pool.tensor_scalar(sr[:, h, :], sr[:, h, :], param(net, "gla_g", h, 1), None, ALU.mult).then_inc(gated, 1)
                for n, t in enumerate(order[1]):
                    pool.wait_ge(ms, n + 1)
                    pool.tensor_tensor(stat[:, 2, t, :], stat[:, 1, t, :], net.half[:, 0:GLA_HEADS], ALU.pow).then_inc(rstd, 1)

            @block.tensor
            def _(pe):
                pe.wait_ge(z_in, 48)
                for n in range(2 * PAIRS):
                    d, c = divmod(n, PAIRS)
                    if n >= 2:
                        pe.wait_ge(z_min, n - 1)
                    for a, z in segs:
                        m = pe.matmul(bank_z[n % 2][:, a:z], wa[:, d, c * P:(c + 1) * P], zt[d][:, a:z], start=True, stop=True)
                    m.then_inc(z_mm, 1)
                pe.wait_ge(z_min, 2 * PAIRS - 1)
                pe.wait_ge(v_in, 16)
                for t in range(NT):
                    if t >= 2:
                        pe.wait_ge(v_ev, t - 1)
                    for h in range(GLA_HEADS):
                        m = pe.transpose(ps_t[t % 2][:, h * P:(h + 1) * P], vf[:, h, t * P:(t + 1) * P], net.ident)
                    m.then_inc(v_tr, 1)
                pe.wait_ge(v_ev, NT)
                pe.wait_ge(masks, 7)

                def turn_kd(d):
                    pe.wait_ge(kd_done, d + 1)
                    if d:
                        pe.wait_ge(o_ev, NT)
                    for g in range(KG):
                        G = d * KG + g
                        if G >= 2:
                            pe.wait_ge(kd_ev, G - 1)
                        for t in (2 * g, 2 * g + 1):
                            for c in range(PAIRS):
                                m = pe.transpose(ps_t[G % 2][:, ((t % 2) * PAIRS + c) * P:((t % 2) * PAIRS + c + 1) * P],
                                                 kd[:, c, t * P:(t + 1) * P], net.ident)
                        m.then_inc(kd_tr, 1)
                    pe.wait_ge(kd_ev, (d + 1) * KG)

                def scores(N, d, t):
                    if N:
                        pe.wait_ge(att_s, 2 * N)
                    for hp in range(2):
                        for c in range(PAIRS):
                            m = pe.matmul(ps_a[hp][:, c * P:(c + 1) * P], kt[hp_rows[hp], c, t * P:(t + 1) * P],
                                          qt[hp_rows[hp], c, t * P:(t + 1) * P], start=True, stop=True)
                    m.then_inc(att_mm, 1)

                def increments(N, d, t):
                    for x, half in enumerate(halves[d]):
                        J = 2 * N + x
                        if J >= 2:
                            pe.wait_ge(st, 4 * (J - 1))
                        rows = hp_rows[half]
                        for h in range(GLA_HEADS):
                            c, hp = divmod(h, 2)
                            m = pe.matmul(ps_d[half][hp_rows[hp], c * DV:(c + 1) * DV], kd_tok[rows, t, h * DK:(h + 1) * DK],
                                          v[rows, t, h * DV:(h + 1) * DV], start=True, stop=True)
                        m.then_inc(ds_mm, 1)

                def outputs(N, d, t):
                    bank = ps_o[N % 2]
                    if 2 <= N < NT:
                        pe.wait_ge(o_ev, N - 1)
                    elif N >= NT + 2:
                        pe.wait_ge(o_sum, N - NT - 1)
                    pe.wait_ge(att_s, 2 * N + 2)
                    for h in range(GLA_HEADS):
                        c, hp = divmod(h, 2)
                        pe.matmul(bank[:, h * DV:(h + 1) * DV], att[N % 2][:, hp, c, :], v[:, t, h * DV:(h + 1) * DV],
                                  start=(h == 0), stop=False, skip_group_check=True)
                    for x, half in enumerate(halves[d]):
                        J = 2 * N + x
                        if J:
                            pe.wait_ge(st, 4 * J)
                        for h in range(GLA_HEADS):
                            m = pe.matmul(bank[hp_rows[half], h * DV:(h + 1) * DV],
                                          qt[:, h // 2, t * P + half * CHUNK:t * P + (half + 1) * CHUNK], state[J % 3][:, h, :],
                                          start=False, stop=(x == 1), skip_group_check=True)
                        m.then_inc(st_pe, 1)
                    pe.wait_ge(st_pe, 2 * N + 2)
                    pe.sem_inc(o_mm, 1)

                def turn_out(n):
                    t = order[1][n]
                    pe.wait_ge(normed, n + 1)
                    if n >= 2:
                        pe.wait_ge(y_ev, n - 1)
                    for h in range(GLA_HEADS):
                        m = pe.transpose(ps_t[n % 2][:, h * P:(h + 1) * P], o[:, t, h * DV:(h + 1) * DV], net.ident)
                    m.then_inc(y_tr, 1)

                for d in range(2):
                    turn_kd(d)
                    pe.wait_ge(kt_done, d + 1)
                    scores(d * NT, d, order[d][0])
                    for n, t in enumerate(order[d]):
                        N = d * NT + n
                        increments(N, d, t)
                        if n + 1 < NT:
                            scores(N + 1, d, order[d][n + 1])
                        outputs(N, d, t)
                        if d and n >= 2:
                            turn_out(n - 2)
                turn_out(NT - 2)
                turn_out(NT - 1)

            @block.scalar
            def _(act):
                for n in range(2 * PAIRS):
                    ba = param(net, "gla_ba", n, 1)
                    act.wait_ge(z_mm, n + 1)
                    act.activation(soft(n), bank_z[n % 2][:, 0:TOK], ACT.Abs, bias=ba).then_inc(z_abs, 1)
                    act.wait_ge(z_abs, n + 1)
                    act.activation(soft(n), soft(n), ACT.Exp, scale=-1.0).then_inc(z_exp, 1)
                for n in range(2 * PAIRS):
                    act.wait_ge(z_exp, n + 1)
                    act.activation(soft(n), soft(n), ACT.Ln, bias=1.0).then_inc(z_ln, 1)
                for t in range(NT):
                    act.wait_ge(v_tr, t + 1)
                    act.activation(v[:, t, :], ps_t[t % 2], ACT.Copy).then_inc(v_ev, 1)
                act.wait_ge(la_done, 2 * PAIRS)
                for d in range(2):
                    act.wait_ge(scanned, 2 * (d + 1))
                    if d:
                        act.wait_ge(kt_done, d)
                        act.wait_ge(st, 4 * NCH)
                    act.activation(e[:], b[:], ACT.Exp, scale=1.0 / TAU).then_inc(e1, 1)
                    act.activation(dec[:].unsqueeze(3), last_of(d), ACT.Exp, scale=1.0 / TAU).then_inc(decs, 1)
                    act.wait_ge(diff, d + 1)
                    act.activation(kd, kd, ACT.Exp, scale=1.0 / TAU).then_inc(e3, 1)
                    act.wait_ge(qt_done, d + 1)
                    act.activation(e[:], b[:], ACT.Exp, scale=-1.0 / TAU).then_inc(e2, 1)
                    for g in range(KG):
                        G = d * KG + g
                        act.wait_ge(kd_tr, G + 1)
                        if d and not g:
                            act.wait_ge(ds_mm, NCH)
                        act.activation(kd_tok[:, 2 * g:2 * g + 2, :], ps_t[G % 2].rearrange("p (t n) -> p t n", t=2),
                                       ACT.Copy).then_inc(kd_ev, 1)
                    if not d:
                        act.wait_ge(r_in, 16)
                        act.activation(sr[:], sr[:], ACT.Silu).then_inc(silu, 1)
                    for n, t in enumerate(order[d]):
                        if d == 0:
                            act.wait_ge(o_mm, n + 1)
                            act.activation(o[:, t, :], ps_o[n % 2], ACT.Copy).then_inc(o_ev, 1)
                        else:
                            act.wait_ge(o_sum, n + 1)
                            for h in range(GLA_HEADS):
                                if n or h:
                                    act.wait_ge(sq, GLA_HEADS * n + h)
                                act.activation(junk[:], o[:, t, h * DV:(h + 1) * DV], ACT.Square,
                                               accum_out=stat[:, 0, t, h:h + 1]).then_inc(sq, 1)

            @block.vector
            def _(dve):
                for n in range(2 * PAIRS):
                    d, c = divmod(n, PAIRS)
                    dve.wait_ge(z_abs, n + 1)
                    dve.tensor_scalar(la[d][:, c, :], bank_z[n % 2][:, 0:TOK], param(net, "gla_ba", n, 1), 0.0, ALU.add, ALU.min)\
                       .then_inc(z_min, 1)
                for n in range(2 * PAIRS):
                    d, c = divmod(n, PAIRS)
                    dve.wait_ge(z_ln, n + 1)
                    dve.wait_ge(z_min, n + 1)
                    dve.tensor_tensor(la[d][:, c, :], la[d][:, c, :], soft(n), ALU.subtract).then_inc(la_done, 1)
                dve.wait_ge(qk_in, 32)
                dve.wait_ge(masks, 7)
                dve.wait_ge(la_done, 2 * PAIRS)
                tri = [net.const[:, CCOL[n]:CCOL[n] + P].unsqueeze(1).to_broadcast([P, PAIRS, P]) for n in ("tri_f", "tri_b")]
                for d in range(2):
                    if d:
                        dve.wait_ge(e2, d)
                    for c in range(PAIRS):
                        rev = slice(None, None, -1) if d else slice(None)
                        dve.tensor_tensor_scan(b[:, c, rev], seg_mask[d][:, rev], la[d][:, c, rev], 0.0, ALU.mult, ALU.add)\
                           .then_inc(scanned, 1)
                    dve.wait_ge(scanned, 2 * (d + 1))
                    if d:
                        dve.wait_ge(kd_tr, KG)
                    else:
                        dve.wait_ge(v_tr, NT)
                    dve.tensor_tensor(chunked(kd), last_of(d).to_broadcast([P, PAIRS, NCH, CHUNK]), chunked(b[:]),
                                      ALU.subtract).then_inc(diff, 1)
                    if d:
                        dve.wait_ge(o_mm, NT)
                    dve.wait_ge(e1, d + 1)
                    dve.scalar_tensor_tensor(qt[:], qf[:], DK ** -0.5, e[:], ALU.mult, ALU.mult).then_inc(qt_done, 1)
                    dve.wait_ge(e3, d + 1)
                    dve.tensor_tensor(kd, kd, kf[:], ALU.mult).then_inc(kd_done, 1)
                    dve.wait_ge(e2, d + 1)
                    dve.tensor_tensor(kt, kf[:], e[:], ALU.mult).then_inc(kt_done, 1)
                    dve.wait_ge(decs, d + 1)

                    def mask(N):
                        dve.wait_ge(att_mm, N + 1)
                        if N >= 2:
                            dve.wait_ge(o_mm, N - 1)
                        for hp in range(2):
                            dve.tensor_tensor(att[N % 2][:, hp], ps_a[hp][:, 0:PAIRS * P].rearrange("p (c q) -> p c q", c=PAIRS),
                                              tri[d], ALU.mult).then_inc(att_s, 1)

                    def finish(n):
                        t = order[1][n]
                        dve.wait_ge(sq, GLA_HEADS * (n + 1))
                        dve.tensor_scalar(stat[:, 1, t, :], stat[:, 0, t, :], 1.0 / DV, EPS, ALU.mult, ALU.add).then_inc(ms, 1)
                        dve.wait_ge(rstd, n + 1)
                        ot = o[:, t, :].rearrange("p (h v) -> p h v", h=GLA_HEADS)
                        dve.tensor_tensor(ot, ot, stat[:, 2, t, :].unsqueeze(2).to_broadcast([P, GLA_HEADS, DV]), ALU.mult)\
                           .then_inc(normed, 1)

                    def gate(n):
                        t = order[1][n]
                        dve.wait_ge(y_tr, n + 1)
                        if not n:
                            dve.wait_ge(gated, GLA_HEADS)
                        place = sr[:, :, t * P:(t + 1) * P]
                        dve.tensor_tensor(place, ps_t[n % 2].rearrange("p (h t) -> p h t", h=GLA_HEADS), place, ALU.mult)\
                           .then_inc(y_ev, 1)

                    mask(d * NT)
                    for n, t in enumerate(order[d]):
                        N = d * NT + n
                        for x, half in enumerate(halves[d]):
                            J = 2 * N + x
                            dve.wait_ge(ds_mm, J + 1)
                            if J >= 2:
                                dve.wait_ge(st_pe, J - 1)
                            if J:
                                dve.wait_ge(st, 4 * J)
                            ci = 2 * t + half
                            for h in range(GLA_HEADS):
                                c, hp = divmod(h, 2)
                                new = state[(J + 1) % 3][hp_rows[hp], h, :]
                                if J + 1 == NCH:
                                    dve.memset(new, 0.0).then_inc(st, 1)
                                else:
                                    dve.scalar_tensor_tensor(new, state[J % 3][hp_rows[hp], h, :], dec[hp_rows[hp], c, ci:ci + 1],
                                                             ps_d[half][hp_rows[hp], c * DV:(c + 1) * DV], ALU.mult, ALU.add)\
                                       .then_inc(st, 1)
                        if n + 1 < NT:
                            mask(N + 1)
                        if d:
                            dve.wait_ge(o_mm, N + 1)
                            dve.tensor_tensor(o[:, t, :], ps_o[N % 2], o[:, t, :], ALU.add).then_inc(o_sum, 1)
                            dve.wait_ge(o_sum, n + 1)
                            if n >= 1:
                                finish(n - 1)
                            if n >= 3:
                                gate(n - 3)
                    if d:
                        gate(NT - 3)
                        finish(NT - 1)
                        gate(NT - 2)
                        gate(NT - 1)


def shared_region(nc, net):
    keep = ExitStack()
    net.regions += 1
    net.region = keep.enter_context(nc.sbuf_tensor(f"region{net.regions}", [P, 8 * TOK], F32))
    return keep


SCRATCH = {"proj0": (IN_AB, TOK), "y0": (D, TOK), "x1": (TOK, D), "hid0": (DFF, TOK), "x2": (TOK, D),
           "proj1": (IN_C, TOK), "y1": (D, TOK), "x3": (LAT, D), "hid1": (DFF, TOK),
           "bias": (NA_HEADS, P, BIAS_COLS), "rpb_rows": (P, P),
           "mod": (DEPTH, 2, 6 * D)}


def trunk(nc, ins, out, scratch):
    net = Net(ins, scratch)
    net.this_stage, net.regions = [], 0
    with ExitStack() as ctx:
        sb = sbuf(nc, ctx)
        net.const = sb("const", [P, N_CONST])
        net.pcol = sb("pcol", [P, N_PCOL])
        net.shift, net.scale = (sb(n, [P, DEPTH, 2, KD, 2]) for n in ("shift", "scale"))
        net.conv = sb("conv", [P, DEPTH, 2 * FT, 4])
        net.half = sb("half", [P, 4])
        net.tile_stored = [ctx.enter_context(nc.semaphore(f"tile_stored{n}")) for n in range(4)]
        net.tiles_stored = [0] * 4
        net.pad_in, net.pad_out, net.slid_in, net.b_stored = (
            ctx.enter_context(nc.semaphore(n)) for n in ("pad_in", "pad_out", "slid_in", "b_stored"))
        net.ident = net.const[:, CCOL["ident"]:CCOL["ident"] + P]
        tiles = lambda ap, n: [ap[t * P:(t + 1) * P, :] for t in range(n)]
        x0 = tiles(net.x[0], LAT_TILES) + tiles(net.ctx[0], CTX_TILES)
        x1, x2 = tiles(net.x1_d, LAT_TILES + CTX_TILES), tiles(net.x2_d, LAT_TILES + CTX_TILES)
        x3, x4 = tiles(net.x3_d, LAT_TILES), tiles(out[0], LAT_TILES)
        setup_stage(nc, net)
        region = shared_region(nc, net)
        project_stage(nc, net, "in0", 0, 0, x0, net.w_in_ab[0], net.proj0_d, "plain", (IN_AB - 2 * RANK) // (2 * P),
                      tail=(IN_AB - P, IN_AB - 2 * RANK), normed=False)
        region.close()
        attention_stage(nc, net, "na", net.proj0_d, net.y0_d, False)
        gla_stage(nc, net, "gla", net.proj0_d, net.y0_d)
        region = shared_region(nc, net)
        close_stage(nc, net, "out0", 0, 0, net.y0_d, net.w_out[0], D, x0, x1)
        project_stage(nc, net, "up0", 0, 1, x1, net.w_up[0], net.hid0_d, "ffn", FT)
        close_stage(nc, net, "down0", 0, 1, net.hid0_d, net.w_down[0], DFF, x1, x2)
        project_stage(nc, net, "in1", 1, 0, x2, net.w_in_c[0], net.proj1_d, "plain", IN_C // (2 * P),
                      early=LAT)
        region.close()
        attention_stage(nc, net, "swa", net.proj1_d, net.y1_d, True)
        region = shared_region(nc, net)
        close_stage(nc, net, "out1", 1, 0, net.y1_d, net.w_out[1], D, x2[:LAT_TILES], x3)
        project_stage(nc, net, "up1", 1, 1, x3, net.w_up[1], net.hid1_d, "ffn", FT)
        close_stage(nc, net, "down1", 1, 1, net.hid1_d, net.w_down[1], DFF, x3, x4, norm_out=False)
        region.close()


_INS = ["x", "c", "ctx", "c_ctx", "w_mod", "b_mod", "g_mix_pre", "g_mix_post", "g_ffn_pre", "g_ffn_post", "w_out", "w_up",
        "conv_w", "conv_b", "w_down", "w_in_ab", "na_rpb", "gla_wa2", "gla_ba", "gla_g", "w_in_c", "swa_sink"]


def constants():
    import numpy as np

    i, j = np.arange(P)[:, None], np.arange(P)[None, :]
    cq, ck = np.arange(P)[:, None] % GRID_W, np.arange(GRID_W)[None, :]
    start = np.clip(cq - NA_WIN // 2, 0, GRID_W - NA_WIN)
    ok = (ck >= start) & (ck < start + NA_WIN)
    same = (i // CHUNK) == (j // CHUNK)
    key = np.arange(3 * P)[None, :] - P
    parts = {
        "ident": i == j,
        "flip": (i < GRID_W) & (j % GRID_W == GRID_W - 1 - i),
        "tri_f": same & (i <= j), "tri_b": same & (i >= j),
        "na_neg": np.where(ok, 0.0, 8 * NEG),
        "four": (i % 32 == np.arange(2)[None, :]),
        "swa_mask": np.where(np.abs(i - key) <= 128, 0.0, 8 * NEG),
    }
    const = np.concatenate([parts[name].astype(np.float32) for name, _ in CONST_COLS], axis=1)
    t = np.arange(LAT)
    inv = (1.0 / (np.float32(10000.0) ** (np.arange(0, HEAD // 2, 2, dtype=np.float32) / np.float32(HEAD // 2)))).astype(np.float32)
    ang = np.concatenate([(t // GRID_W).astype(np.float32)[:, None] * inv, (t % GRID_W).astype(np.float32)[:, None] * inv], -1)
    cos, sin = np.cos(ang).T, np.sin(ang).T
    pair = (np.arange(P) % HEAD) // 2
    sign = np.where(np.arange(P) % 2 == 0, -1.0, 1.0)[:, None]
    rope = np.stack([cos[pair], sin[pair] * sign]).astype(np.float32)
    return const, rope


def kernel(**inputs):
    import numpy as np
    import concourse.bacc as bacc
    from concourse.bass_utils import run_bass_kernel_spmd

    nc = bacc.Bacc("TRN2", target_bir_lowering=False, num_devices=1)
    const, rope = constants()
    arrays = {f"in_{n}": np.ascontiguousarray(inputs[n]) for n in _INS}
    arrays["in_const_d"], arrays["in_rope_d"] = const, rope
    ins = {n[3:]: nc.dram_tensor(n, a.shape, mybir.dt.from_np(a.dtype), kind="ExternalInput").ap() for n, a in arrays.items()}
    scratch = {n: nc.dram_tensor(f"scratch_{n}", shape, F32, kind="Internal").ap() for n, shape in SCRATCH.items()}
    out = nc.dram_tensor("out_0", (1, LAT, D), F32, kind="ExternalOutput").ap()
    trunk(nc, ins, out, scratch)
    r = run_bass_kernel_spmd(nc, [arrays], core_ids=[0])
    return r.results[0]["out_0"]
```
